# Optimizing a Trainium2 kernel written in Bass

```python
import jax, jax.numpy as jnp
from jax import lax
import numpy as np

D_MODEL = 1024
BATCH = 1
SEQ = 512
DEPTH = 2

GRID_W = 64
CTX_LEN = 256
MIX_WIDTH = D_MODEL
CONV_A_WIDTH = D_MODEL // 4
CONV_A_K = 3
CONV_B_WIDTH = D_MODEL // 4
CONV_B_K = 31
MLA_HEADS = 8
QK_NOPE = 64
QK_ROPE = 32
V_DIM = 64
Q_LORA = 256
KV_LORA = 128
MLA_WIDTH = MLA_HEADS * V_DIM
PROJ_WIDTH = 3 * CONV_A_WIDTH + 2 * CONV_B_WIDTH + Q_LORA + KV_LORA + QK_ROPE
ATTN_SCALE = (QK_NOPE + QK_ROPE) ** -0.5
Q_BLOCK = 128
ROPE_BASE = 10000.0
PEER_HEADS = 8
N_KEYS = 128
N_EXPERTS = N_KEYS * N_KEYS
PK_HALF = 128
PEER_TOPK = 16
PEER_CHUNK = 128
EPS = 1e-6

kernel_name = "hybrid_conv_mla_peer_diffusion_trunk"

def rmsnorm(x, g):
    xf = x.astype(jnp.float32)
    y = xf * lax.rsqrt(jnp.mean(xf * xf, axis=-1, keepdims=True) + EPS)
    return (y * g.astype(jnp.float32)).astype(x.dtype)

def layernorm(x, g, b):
    xf = x.astype(jnp.float32)
    mu = jnp.mean(xf, axis=-1, keepdims=True)
    var = jnp.mean(jnp.square(xf - mu), axis=-1, keepdims=True)
    y = (xf - mu) * lax.rsqrt(var + EPS)
    return (y * g.astype(jnp.float32) + b.astype(jnp.float32)).astype(x.dtype)

def dwconv(x, w):
    return lax.conv_general_dilated(
        x, w.astype(x.dtype)[:, None, :], window_strides=(1,), padding='SAME',
        dimension_numbers=('NWC', 'WIO', 'NWC'), feature_group_count=x.shape[-1])

def split_proj(p):
    widths = (CONV_A_WIDTH, CONV_A_WIDTH, CONV_A_WIDTH, 2 * CONV_B_WIDTH, Q_LORA, KV_LORA, QK_ROPE)
    points, acc = [], 0
    for w in widths[:-1]:
        acc += w
        points.append(acc)
    return jnp.split(p, points, axis=-1)

def conv_mixers(a_b, a_c, a_h, glu_in, conv_a_w, conv_b_w, conv_b_bias, ln_g, ln_b):
    y_a = a_b * dwconv(a_c * a_h, conv_a_w)
    g_a, g_b = jnp.split(glu_in, 2, axis=-1)
    u = dwconv(g_a * jax.nn.sigmoid(g_b), conv_b_w) + conv_b_bias
    y_b = jax.nn.silu(layernorm(u, ln_g, ln_b))
    return jnp.concatenate([y_a, y_b], axis=-1)

def mla_q(p_q, g, w_uq):
    q = (rmsnorm(p_q, g) @ w_uq).reshape(*p_q.shape[:-1], MLA_HEADS, QK_NOPE + QK_ROPE)
    return q[..., :QK_NOPE], q[..., QK_NOPE:]

def mla_kv(p_kv, g, w_ukv):
    kv = (rmsnorm(p_kv, g) @ w_ukv).reshape(*p_kv.shape[:-1], MLA_HEADS, QK_NOPE + V_DIM)
    return kv[..., :QK_NOPE], kv[..., QK_NOPE:]

def rotate_half(seg):
    h = seg.shape[-1] // 2
    return jnp.concatenate([-seg[..., h:], seg[..., :h]], axis=-1)

def apply_rope2d(x, cos, sin):
    half = QK_ROPE // 2
    rot = jnp.concatenate([rotate_half(x[..., :half]), rotate_half(x[..., half:])], axis=-1)
    return x * cos.astype(x.dtype) + rot * sin.astype(x.dtype)

def rope2d_tables(n):
    rows = n // GRID_W
    row = jnp.repeat(jnp.arange(rows, dtype=jnp.float32), GRID_W)
    col = jnp.tile(jnp.arange(GRID_W, dtype=jnp.float32), rows)
    axis_dim = QK_ROPE // 2
    inv = ROPE_BASE ** (-jnp.arange(0, axis_dim, 2, dtype=jnp.float32) / axis_dim)
    ar = row[:, None] * inv[None, :]
    ac = col[:, None] * inv[None, :]
    ang = jnp.concatenate([ar, ar, ac, ac], axis=-1)
    return jnp.cos(ang), jnp.sin(ang)

def join_qk(nope, rope_part):
    if rope_part.ndim == nope.ndim - 1:
        rope_part = jnp.broadcast_to(rope_part[..., None, :], nope.shape[:-1] + (QK_ROPE,))
    return jnp.concatenate([nope, rope_part], axis=-1)

def attend(q, k, v):
    s = jnp.einsum('bqhd,bkhd->bhqk', q, k).astype(jnp.float32) * ATTN_SCALE
    p = jax.nn.softmax(s, axis=-1)
    return jnp.einsum('bhqk,bkhd->bqhd', p.astype(v.dtype), v)

def latent_attention(q, k, v):
    b, n = q.shape[0], q.shape[1]
    nb = n // Q_BLOCK
    qb = q.reshape(b, nb, Q_BLOCK, MLA_HEADS, q.shape[-1]).transpose(1, 0, 2, 3, 4)
    out = lax.map(lambda qi: attend(qi, k, v), qb)
    return out.transpose(1, 0, 2, 3, 4).reshape(b, n, MLA_WIDTH)

def peer_ffn(h, w_q, sub_keys, u, v):
    b, l, d = h.shape
    hb = h.reshape(-1, PEER_CHUNK, d)

    def chunk(ht):
        q = (ht @ w_q).reshape(PEER_CHUNK, PEER_HEADS, 2, PK_HALF)
        s = jnp.einsum('thpd,hpkd->thpk', q, sub_keys).astype(jnp.float32)
        top_s, top_i = lax.top_k(s, PEER_TOPK)
        cand_s = (top_s[:, :, 0, :, None] + top_s[:, :, 1, None, :]).reshape(PEER_CHUNK, PEER_HEADS, -1)
        cand_i = (top_i[:, :, 0, :, None] * N_KEYS + top_i[:, :, 1, None, :]).reshape(PEER_CHUNK, PEER_HEADS, -1)
        best_s, best_p = lax.top_k(cand_s, PEER_TOPK)
        idx = jnp.take_along_axis(cand_i, best_p, axis=-1)
        gate = jax.nn.softmax(best_s, axis=-1)
        act = jnp.einsum('thkd,td->thk', u[idx], ht).astype(jnp.float32)
        wts = (jax.nn.gelu(act, approximate=False) * gate).astype(ht.dtype)
        return jnp.einsum('thk,thkd->td', wts, v[idx])

    return lax.map(chunk, hb).reshape(b, l, d)

def setup_inputs(seed: int = 0) -> dict:
    key = jax.random.key(seed)
    ks = jax.random.split(key, 24)
    f = jnp.float32
    nrm = lambda k, shape, s: jax.random.normal(k, shape, f) * s
    D = D_MODEL
    return {
        "x": nrm(ks[0], (BATCH, SEQ, D), 1.0),
        "c": nrm(ks[1], (BATCH, D), 1.0),
        "ctx": nrm(ks[2], (BATCH, CTX_LEN, D), 1.0),
        "c_ctx": nrm(ks[3], (D,), 1.0),
        "w_mod": nrm(ks[4], (DEPTH, D, 6 * D), 0.5 * D ** -0.5),
        "b_mod": nrm(ks[5], (DEPTH, 6 * D), 0.02),
        "norm1_g": 1.0 + nrm(ks[6], (DEPTH, D), 0.02),
        "norm2_g": 1.0 + nrm(ks[7], (DEPTH, D), 0.02),
        "w_in": nrm(ks[8], (DEPTH, D, PROJ_WIDTH), D ** -0.5),
        "w_out": nrm(ks[9], (DEPTH, MIX_WIDTH, D), MIX_WIDTH ** -0.5),
        "conv_a_w": nrm(ks[10], (DEPTH, CONV_A_K, CONV_A_WIDTH), CONV_A_K ** -0.5),
        "conv_b_w": nrm(ks[11], (DEPTH, CONV_B_K, CONV_B_WIDTH), CONV_B_K ** -0.5),
        "conv_b_bias": nrm(ks[12], (DEPTH, CONV_B_WIDTH), 0.02),
        "conv_b_ln_g": 1.0 + nrm(ks[13], (DEPTH, CONV_B_WIDTH), 0.02),
        "conv_b_ln_b": nrm(ks[14], (DEPTH, CONV_B_WIDTH), 0.02),
        "mla_q_norm_g": 1.0 + nrm(ks[15], (DEPTH, Q_LORA), 0.02),
        "w_uq": nrm(ks[16], (DEPTH, Q_LORA, MLA_HEADS * (QK_NOPE + QK_ROPE)), Q_LORA ** -0.5),
        "mla_kv_norm_g": 1.0 + nrm(ks[17], (DEPTH, KV_LORA), 0.02),
        "w_ukv": nrm(ks[18], (DEPTH, KV_LORA, MLA_HEADS * (QK_NOPE + V_DIM)), KV_LORA ** -0.5),
        "peer_w_q": nrm(ks[19], (DEPTH, D, PEER_HEADS * 2 * PK_HALF), D ** -0.5),
        "peer_sub_keys": nrm(ks[20], (DEPTH, PEER_HEADS, 2, N_KEYS, PK_HALF), PK_HALF ** -0.5),
        "peer_u": nrm(ks[21], (DEPTH, N_EXPERTS, D), D ** -0.5),
        "peer_v": nrm(ks[22], (DEPTH, N_EXPERTS, D), PEER_HEADS ** -0.5),
        "final_norm_g": 1.0 + nrm(ks[23], (D,), 0.02),
    }

def reference(x, c, ctx, c_ctx, w_mod, b_mod, norm1_g, norm2_g, w_in, w_out, conv_a_w, conv_b_w,
              conv_b_bias, conv_b_ln_g, conv_b_ln_b, mla_q_norm_g, w_uq, mla_kv_norm_g, w_ukv,
              peer_w_q, peer_sub_keys, peer_u, peer_v, final_norm_g):
    n = x.shape[1]
    cos, sin = rope2d_tables(n)
    cos_q, sin_q = cos[None, :, None, :], sin[None, :, None, :]
    cos_k, sin_k = cos[None, :, :], sin[None, :, :]
    silu_c = jax.nn.silu(c)
    silu_cc = jax.nn.silu(c_ctx)

    for l in range(DEPTH):
        last = l == DEPTH - 1
        sh1, sc1, g1, sh2, sc2, g2 = jnp.split((silu_c @ w_mod[l] + b_mod[l])[:, None, :], 6, axis=-1)
        csh1, csc1, cg1, csh2, csc2, cg2 = jnp.split(silu_cc @ w_mod[l] + b_mod[l], 6, axis=-1)

        hx = rmsnorm(x, norm1_g[l]) * (1 + sc1) + sh1
        hc = rmsnorm(ctx, norm1_g[l]) * (1 + csc1) + csh1
        xa_b, xa_c, xa_h, x_glu, x_q, x_kv, x_kr = split_proj(hx @ w_in[l])
        ca_b, ca_c, ca_h, c_glu, c_q, c_kv, c_kr = split_proj(hc @ w_in[l])

        kn_c, v_c = mla_kv(c_kv, mla_kv_norm_g[l], w_ukv[l])
        k_c = join_qk(kn_c, c_kr)

        qn_x, qr_x = mla_q(x_q, mla_q_norm_g[l], w_uq[l])
        kn_x, v_x = mla_kv(x_kv, mla_kv_norm_g[l], w_ukv[l])
        q_x = join_qk(qn_x, apply_rope2d(qr_x, cos_q, sin_q))
        k_x = join_qk(kn_x, apply_rope2d(x_kr, cos_k, sin_k))
        att_x = latent_attention(q_x, jnp.concatenate([k_x, k_c], axis=1), jnp.concatenate([v_x, v_c], axis=1))

        conv_x = conv_mixers(xa_b, xa_c, xa_h, x_glu, conv_a_w[l], conv_b_w[l], conv_b_bias[l],
                             conv_b_ln_g[l], conv_b_ln_b[l])
        x = x + g1 * (jnp.concatenate([conv_x, att_x], axis=-1) @ w_out[l])

        if not last:
            qn_c, qr_c = mla_q(c_q, mla_q_norm_g[l], w_uq[l])
            att_c = attend(join_qk(qn_c, qr_c), k_c, v_c).reshape(ctx.shape[0], ctx.shape[1], MLA_WIDTH)
            conv_c = conv_mixers(ca_b, ca_c, ca_h, c_glu, conv_a_w[l], conv_b_w[l], conv_b_bias[l],
                                 conv_b_ln_g[l], conv_b_ln_b[l])
            ctx = ctx + cg1 * (jnp.concatenate([conv_c, att_c], axis=-1) @ w_out[l])

        hx2 = rmsnorm(x, norm2_g[l]) * (1 + sc2) + sh2
        x = x + g2 * peer_ffn(hx2, peer_w_q[l], peer_sub_keys[l], peer_u[l], peer_v[l])
        if not last:
            hc2 = rmsnorm(ctx, norm2_g[l]) * (1 + csc2) + csh2
            ctx = ctx + cg2 * peer_ffn(hc2, peer_w_q[l], peer_sub_keys[l], peer_u[l], peer_v[l])

    return rmsnorm(x, final_norm_g)


_drawn_inputs = setup_inputs


def setup_inputs(seed=0):
    import zlib

    import numpy as np

    out = dict(_drawn_inputs(seed))
    spreads = {}
    factors = {'ctx': 4.195,
     'norm1_g': 4.532,
     'norm2_g': 36.224,
     'conv_b_bias': 62.928,
     'conv_b_ln_g': 64.0,
     'conv_b_ln_b': 64.0,
     'mla_q_norm_g': 8.0,
     'mla_kv_norm_g': 8.0,
     'final_norm_g': 8.587}
    for name, (base, spread) in spreads.items():
        noise = np.random.default_rng([zlib.crc32(name.encode()), seed]).standard_normal(out[name].shape)
        drawn = base * np.exp(spread * noise) if base else spread * noise
        out[name] = __import__('jax').numpy.asarray(drawn.astype(out[name].dtype))
    for name, factor in factors.items():
        out[name] = (out[name] * factor).astype(out[name].dtype)
    return out
```

```python
from contextlib import ExitStack

import numpy as np

import concourse.bass as bass
from concourse import mybir

F32 = mybir.dt.float32
U32 = mybir.dt.uint32
ALU = mybir.AluOpType
ACT = mybir.ActivationFunctionType
AX_X = mybir.AxisListType.X

P = 128
D = 1024
KD = D // P
DEPTH = 2
SEQ, CTX = 512, 256
TOK = SEQ + CTX
NX, NT = SEQ // P, TOK // P
HEADS, NOPE, ROPE, VD = 8, 64, 32, 64
QK = NOPE + ROPE
SCALE = QK ** -0.5
CONV_A, CONV_B = 3, 31
PAD_A, PAD_B = CONV_A // 2, CONV_B // 2
QCHUNK, KVCHUNK, KRCHUNK = 10, 12, 13
NPROJ = 13
EPS = 1e-6
PH, NKEY, TOPK = 8, 128, 16
LOWEST = -3.0e38
BLOCK = 4
NU = NV = 8
SLABS = 3
GRID_W, ROPE_BASE = 64, 10000.0


class Links:

    def __init__(self, eng, sem):
        self.eng, self.sem, self.n = eng, sem, 0

    def mark(self, ins):
        self.n += 1
        ins.then_inc(self.sem, 1)

    def wait(self, behind=0):
        if self.n > behind:
            self.eng.wait_ge(self.sem, self.n - behind)

    def __call__(self, ins):
        self.mark(ins)
        self.wait()

    def reset(self):
        self.wait()
        if self.n:
            self.eng.sem_clear(self.sem)
        self.n = 0


class Program:

    def __init__(self, nc, stack, a):
        self.nc, self.stack, self.a = nc, stack, a
        sb = self.sb
        self.x = sb("x_tiles", [P, NT + 1, D])
        self.rows = sb("mod_rows", [P, 2, 3, D])
        self.ident = sb("ident", [P, P])
        self.ones = sb("ones", [P, P])
        self.rope = sb("rope", [P, 2, SEQ])
        self.half = sb("minus_half", [P, NT])
        self.iota = sb("iota16", [P, TOPK])
        self.cols = sb("cols", [P, 2, 38])
        self.kvg = sb("kv_norm_g", [P, 1])
        self.ps = stack.enter_context(nc.psum_tensor("psum", [P, 8, 512], F32))
        self.mod_dram = nc.dram_tensor("mod_dram", (2, DEPTH * 6 * D), F32, kind="Internal").ap()
        self.dve_step = stack.enter_context(nc.semaphore("dve_step"))

    def sb(self, name, shape, dt=F32):
        return self.stack.enter_context(self.nc.sbuf_tensor(name, shape, dt))

    def sem(self, name):
        self.phase_sems.append(self.sem_stack.enter_context(self.nc.semaphore(name)))
        return self.phase_sems[-1]

    def sems(self, tag, *names):
        return [self.sem(f"{n}_{tag}") for n in names]

    def psum2(self, b):
        return self.ps[:, 2 * b:2 * b + 2, :].rearrange("p b n -> p (b n)")


def phase(build):
    def run(g, *args):
        with ExitStack() as g.sem_stack:
            g.phase_sems = []
            build(g, *args)
            numbers = sorted(x.num for x in g.phase_sems)
            starts = [n for n in numbers if n - 1 not in numbers]
            ends = [n + 1 for n in numbers if n + 1 not in numbers]
            for first, end in zip(starts, ends):
                g.nc.gpsimd.sem_clear(range(first, end))
            g.nc.all_engine_barrier()
    return run


@phase
def modulation(g):
    nc, a = g.nc, g.a
    NCH = 6 * D // 512
    tensors_loaded, c_ready, row_done, row_added, rows_out = g.sems("m", "tensors_loaded", "c_ready", "row_done",
                                                                     "row_added", "rows_out")
    c_loaded, zeroed, bias_loaded = g.sems("m", "c_loaded", "zeroed", "bias_loaded")
    slab_loaded = [g.sem(f"slab_loaded_m{r}") for r in range(SLABS)]
    with ExitStack() as s:
        sb = lambda n, shape: s.enter_context(nc.sbuf_tensor(n, shape, F32))
        slab = sb("mod_slab", [P, SLABS, KD, 512])
        c = sb("c_cols", [P, KD, 2])
        e = sb("c_exp", [P, KD, 2])
        bias = sb("mod_bias", [2, DEPTH * 6 * D])
        rows = sb("mod_out", [2, DEPTH * 6 * D])
        with nc.Block() as block:
            @block.sync
            def _(sp):
                with nc.allow_non_contiguous_dma(reason="a vector onto partitions"):
                    sp.dma_start(c[:, :, 0], a["c"].rearrange("b (k p) -> p (b k)", p=P)).then_inc(c_loaded, 16)
                    sp.dma_start(c[:, :, 1], a["c_ctx"].rearrange("(k p) -> p k", p=P)).then_inc(c_loaded, 16)
                sp.dma_start(bias[:], a["b_mod"].rearrange("l n -> (l n)").partition_broadcast(2)).then_inc(bias_loaded, 16)
                for l in range(DEPTH):
                    w = a["w_mod"][l].rearrange("(k p) n -> p k n", p=P)
                    with sp.Fori(0, NCH // SLABS) as i:
                        for r in range(SLABS):
                            sp.wait_ge(row_done, i * SLABS + (l * NCH + r + 1))
                            sp.dma_start(slab[:, r], w[:, :, bass.ds(i * (SLABS * 512) + r * 512, 512)]
                                         ).then_inc(slab_loaded[r], 16)
                    if l == 0:
                        sp.dma_start(g.x[:, 1:NX + 1], a["x"].rearrange("b (t p) d -> p (b t) d", p=P)
                                     ).then_inc(tensors_loaded, 16)
                        sp.dma_start(g.x[:, NX + 1:], a["ctx"].rearrange("b (t p) d -> p (b t) d", p=P)
                                     ).then_inc(tensors_loaded, 16)
                        sp.dma_start(g.ident[:], a["identity"]).then_inc(tensors_loaded, 16)
                        sp.dma_start(g.rope[NOPE:QK], a["rope_tables"]).then_inc(tensors_loaded, 16)
                sp.wait_ge(row_added, DEPTH * NCH + SLABS)
                sp.dma_start(g.mod_dram, rows[:]).then_inc(rows_out, 16)
                sp.wait_ge(rows_out, 16)
                sp.wait_ge(tensors_loaded, 64)

            @block.gpsimd
            def _(pool):
                pool.memset(g.ones[:], 1.0)
                pool.memset(g.half[:], -0.5)
                pool.memset(g.x[:, 0], 0.0)
                pool.iota(g.iota[:], [[1, TOPK]], base=0, channel_multiplier=0,
                          allow_small_or_imprecise_dtypes=True)

            @block.scalar
            def _(act):
                act.wait_ge(c_loaded, 32)
                act.activation(e[:], c[:], ACT.Exp, scale=-1.0).then_inc(zeroed, 1)

            @block.vector
            def _(dve):
                link = Links(dve, g.dve_step)
                dve.sem_inc(row_added, SLABS)
                dve.wait_ge(zeroed, 1)
                link(dve.tensor_scalar(e[:], e[:], 1.0, None, ALU.add))
                link(dve.reciprocal(e[:], e[:]))
                dve.tensor_tensor(c[:], c[:], e[:], ALU.mult).then_inc(c_ready, 1)
                dve.wait_ge(bias_loaded, 16)
                for l in range(DEPTH):
                    with dve.Fori(0, NCH // SLABS) as i:
                        for r in range(SLABS):
                            at = bass.ds(i * (SLABS * 512) + (l * NCH + r) * 512, 512)
                            dve.wait_ge(row_done, i * SLABS + (l * NCH + r + 1 + SLABS))
                            dve.tensor_tensor(rows[:, at], g.ps[0:2, r, :], bias[:, at], ALU.add).then_inc(row_added, 1)
                link.reset()

            @block.tensor
            def _(pe):
                pe.sem_inc(row_done, SLABS)
                pe.wait_ge(c_ready, 1)
                for l in range(DEPTH):
                    with pe.Fori(0, NCH // SLABS) as i:
                        for r in range(SLABS):
                            pe.wait_ge(slab_loaded[r], i * 16 + 16 * (l * NCH // SLABS + 1))
                            pe.wait_ge(row_added, i * SLABS + (l * NCH + r + 1))
                            for k in range(KD):
                                last = pe.matmul(g.ps[0:2, r, :], c[:, k, :], slab[:, r, k, :],
                                                 start=(k == 0), stop=(k == KD - 1))
                            last.then_inc(row_done, 1)


def load_mod_rows(g, sp, l, which, loaded):
    at = (l * 6 + which * 3) * D
    for s in range(2):
        sp.dma_start(g.rows[:, s].rearrange("p r n -> p (r n)"),
                     g.mod_dram[s, at:at + 3 * D].partition_broadcast(P)).then_inc(loaded, 16)


@phase
def norm_and_project(g, l, which, tiles, h, out):
    nc, a = g.nc, g.a
    tag = f"{l}{which}"
    rows_loaded, squared, mean_ready, rstd_ready, h_ready, transposed, ht_ready, chunk_done, chunk_copied = g.sems(
        tag, "rows_loaded", "squared", "mean_ready", "rstd_ready", "h_ready", "transposed", "ht_ready",
        "chunk_done", "chunk_copied")
    rot_slab_ready, keys_loaded, rope_in, cols_loaded = g.sems(tag, "rot_slab_ready", "keys_loaded", "rope_in", "cols_loaded")
    slab_loaded = [g.sem(f"slab_loaded_{tag}{r}") for r in range(2)]
    w = (a["w_in"] if which == 0 else a["peer_w_q"])[l].rearrange("(k p) n -> p k n", p=P)
    norm_g = (a["norm1_g"] if which == 0 else a["norm2_g"])[l]
    looped = 12 if which == 0 else 2 * PH
    tokens = tiles * P
    wide = SEQ if which == 0 and l == DEPTH - 1 else tokens
    with ExitStack() as s:
        sb = lambda n, shape: s.enter_context(nc.sbuf_tensor(f"{n}_{tag}", shape, F32))
        grow = sb("norm_g_row", [P, D])
        ht = sb("h_t", [P, KD, tokens])
        slab = sb("slab", [P, 2, KD, P])
        stat = sb("stat", [P, 3, NT])
        if which == 0:
            rot_slab = sb("rot_slab", [P, KD, QK])
            kr_raw = sb("kr_raw", [P, TOK])
            kr_rot = sb("kr_rot", [P, SEQ])
        else:
            keys = sb("sub_keys", [P, 2 * PH, P])

        def stream(t):
            return 0 if t < NX else 1

        with nc.Block() as block:
            @block.sync
            def _(sp):
                load_mod_rows(g, sp, l, which, rows_loaded)
                sp.dma_start(grow[:], norm_g.partition_broadcast(P)).then_inc(rows_loaded, 16)
                if which == 1:
                    sp.dma_start(keys[:], a["peer_sub_keys"][l].rearrange("h p k d -> k (h p) d")).then_inc(keys_loaded, 16)
                with sp.Fori(0, looped // 2) as i:
                    for r in range(2):
                        sp.wait_ge(chunk_done, i * 2 + (r + 1))
                        sp.dma_start(slab[:, r], w[:, :, bass.ds(i * (2 * P) + r * P, P)]).then_inc(slab_loaded[r], 16)
                if which == 0:
                    sp.wait_ge(chunk_done, looped + 1)
                    sp.dma_start(slab[:, 0], w[:, :, KVCHUNK * P:(KVCHUNK + 1) * P]).then_inc(slab_loaded[0], 16)
                    sp.wait_ge(chunk_done, looped + 2)
                    sp.dma_start(slab[:, 1, :, 0:QK], w[:, :, KRCHUNK * P - NOPE:]).then_inc(slab_loaded[1], 16)
                    with nc.allow_non_contiguous_dma(reason="vectors onto partitions"):
                        col = lambda name: a[name][l].rearrange("(c p) -> p c", p=P)
                        sp.dma_start(g.cols[:, :, 34], col("conv_b_bias")).then_inc(cols_loaded, 16)
                        sp.dma_start(g.cols[:, :, 35], col("conv_b_ln_g")).then_inc(cols_loaded, 16)
                        sp.dma_start(g.cols[:, :, 36], col("conv_b_ln_b")).then_inc(cols_loaded, 16)
                        sp.dma_start(g.cols[:, :, 37], col("mla_q_norm_g")).then_inc(cols_loaded, 16)
                        sp.dma_start(g.kvg[:], col("mla_kv_norm_g")).then_inc(cols_loaded, 16)
                        for c in range(2):
                            sp.dma_start(g.cols[:, c, 0:CONV_A], a["conv_a_w"][l][:, c * P:(c + 1) * P].rearrange(
                                "k p -> p k")).then_inc(cols_loaded, 16)
                            sp.dma_start(g.cols[:, c, CONV_A:CONV_A + CONV_B], a["conv_b_w"][l][:, c * P:(c + 1) * P].rearrange(
                                "k p -> p k")).then_inc(cols_loaded, 16)
                    sp.wait_ge(cols_loaded, 16 * 9)

            @block.scalar
            def _(act):
                act.sem_inc(chunk_copied, 2)
                for t in range(tiles):
                    act.activation(h[:, t], g.x[:, t + 1], ACT.Square, accum_out=stat[:, 0, t:t + 1]).then_inc(squared, 1)
                for t in range(tiles):
                    act.wait_ge(transposed, t + 1)
                    act.activation(ht[:, :, t * P:(t + 1) * P], g.psum2(t % 2).rearrange("p (k n) -> p k n", k=KD),
                                   ACT.Copy).then_inc(ht_ready, 1)
                if which == 1:
                    for b in range(2):
                        act.wait_ge(transposed, tiles + b + 1)
                        act.activation(out["keys_t"][:, b * KD:(b + 1) * KD], g.psum2(2 + b).rearrange(
                            "p (k n) -> p k n", k=KD), ACT.Copy).then_inc(ht_ready, 1)
                with act.Fori(0, looped // 2) as i:
                    for r in range(2):
                        act.wait_ge(chunk_done, i * 2 + (r + 3))
                        act.activation(out["proj"][:, bass.ds(i * 2 + r, 1), 0:wide].rearrange("p c n -> p (c n)"),
                                       g.psum2(r)[:, 0:wide], ACT.Copy).then_inc(chunk_copied, 1)
                if which == 0:
                    act.wait_ge(chunk_done, looped + 3)
                    act.activation(out["proj"][:, KVCHUNK], g.psum2(0)[:, 0:TOK], ACT.Copy).then_inc(chunk_copied, 1)
                    act.wait_ge(chunk_done, looped + 4)
                    act.activation(kr_raw[NOPE:QK], g.psum2(1)[NOPE:QK, 0:TOK], ACT.Copy).then_inc(rope_in, 1)
                    act.wait_ge(chunk_done, looped + 5)
                    act.activation(kr_rot[NOPE:QK], g.psum2(2)[NOPE:QK, 0:SEQ], ACT.Copy).then_inc(rope_in, 1)

            @block.gpsimd
            def _(pool):
                pool.wait_ge(mean_ready, 1)
                pool.tensor_tensor(stat[:, 2, 0:tiles], stat[:, 1, 0:tiles], g.half[:, 0:tiles], ALU.pow).then_inc(rstd_ready, 1)
                if which == 0:
                    pool.memset(rot_slab[:], 0.0).then_inc(rot_slab_ready, 1)

            @block.vector
            def _(dve):
                link = Links(dve, g.dve_step)
                dve.wait_ge(rows_loaded, 48)
                for st in range(2):
                    link(dve.scalar_tensor_tensor(g.rows[:, st, 1], g.rows[:, st, 1], 1.0, grow[:], ALU.add, ALU.mult))
                dve.wait_ge(squared, tiles)
                dve.tensor_scalar(stat[:, 1, 0:tiles], stat[:, 0, 0:tiles], 1.0 / D, EPS, ALU.mult, ALU.add
                                  ).then_inc(mean_ready, 1)
                dve.wait_ge(rstd_ready, 1)
                for t in range(tiles):
                    link(dve.scalar_tensor_tensor(h[:, t], g.x[:, t + 1], stat[:, 2, t:t + 1], g.rows[:, stream(t), 1],
                                                  ALU.mult, ALU.mult))
                    dve.tensor_tensor(h[:, t], h[:, t], g.rows[:, stream(t), 0], ALU.add).then_inc(h_ready, 1)
                if which == 0:
                    dve.wait_ge(rot_slab_ready, 1)
                    dve.wait_ge(slab_loaded[1], 16 * (looped // 2 + 1))
                    src = slab[:, 1, :, NOPE:QK].rearrange("p k (s u e) -> p k s u e", s=2, u=2)
                    dst = rot_slab[:, :, NOPE:QK].rearrange("p k (s u e) -> p k s u e", s=2, u=2)
                    link.mark(dve.tensor_scalar(dst[:, :, :, 0], src[:, :, :, 1], -1.0, None, ALU.mult))
                    dve.tensor_copy(dst[:, :, :, 1], src[:, :, :, 0]).then_inc(rot_slab_ready, 1)
                    link.wait()
                    dve.wait_ge(rope_in, 2)
                    kr = slice(NOPE, QK)
                    link(dve.tensor_tensor(kr_rot[kr], kr_rot[kr], g.rope[kr, 1], ALU.mult))
                    for e in range(2):
                        kt = out["k_t"]
                        link.mark(dve.tensor_copy(kt[kr, e, SEQ:], kr_raw[kr, SEQ:]))
                        link(dve.tensor_tensor(kt[kr, e, 0:SEQ], kr_raw[kr, 0:SEQ], g.rope[kr, 0], ALU.mult))
                        link(dve.tensor_tensor(kt[kr, e, 0:SEQ], kt[kr, e, 0:SEQ], kr_rot[kr], ALU.add))
                link.reset()

            @block.tensor
            def _(pe):
                pe.sem_inc(chunk_done, 2)

                def chunk(psum, lhs, m, n_tok):
                    for k in range(KD):
                        for at in range(0, n_tok, 512):
                            to = min(at + 512, n_tok)
                            last = pe.matmul(psum[0:m, at:to], lhs[:, k, 0:m], ht[:, k, at:to],
                                             start=(k == 0), stop=(k == KD - 1))
                    last.then_inc(chunk_done, 1)

                for t in range(tiles):
                    pe.wait_ge(h_ready, t + 1)
                    if t >= 2:
                        pe.wait_ge(ht_ready, t - 1)
                    for k in range(KD):
                        last = pe.transpose(g.psum2(t % 2)[:, k * P:(k + 1) * P], h[:, t, k * P:(k + 1) * P], g.ident[:])
                    last.then_inc(transposed, 1)
                if which == 1:
                    pe.wait_ge(keys_loaded, 16)
                    for b in range(2):
                        for k in range(KD):
                            last = pe.transpose(g.psum2(2 + b)[:, k * P:(k + 1) * P], keys[:, b * KD + k], g.ident[:])
                        last.then_inc(transposed, 1)
                pe.wait_ge(ht_ready, tiles)
                with pe.Fori(0, looped // 2) as i:
                    for r in range(2):
                        pe.wait_ge(slab_loaded[r], i * 16 + 16)
                        pe.wait_ge(chunk_copied, i * 2 + (r + 1))
                        chunk(g.psum2(r), slab[:, r], P, wide)
                if which == 0:
                    pe.wait_ge(slab_loaded[0], 16 * (looped // 2 + 1))
                    pe.wait_ge(chunk_copied, looped + 1)
                    chunk(g.psum2(0), slab[:, 0], P, TOK)
                    pe.wait_ge(slab_loaded[1], 16 * (looped // 2 + 1))
                    pe.wait_ge(chunk_copied, looped + 2)
                    chunk(g.psum2(1), slab[:, 1], QK, TOK)
                    pe.wait_ge(rot_slab_ready, 2)
                    chunk(g.psum2(2), rot_slab, QK, SEQ)


@phase
def mix(g, l, proj, k_t, cat):
    nc, a = g.nc, g.a
    tag = f"{l}x"
    last_layer = l == DEPTH - 1
    tiles = NX if last_layer else NT
    W = tiles * P
    WA = W if last_layer else W + PAD_A
    WB = W if last_layer else W + PAD_B
    latent_squared, latent_summed, latent_mean, latent_root, latent_ready = g.sems(
        tag, "latent_squared", "latent_summed", "latent_mean", "latent_root", "latent_ready")
    v_done, v_copied, kv_loaded, padded, sigmoid_ready = g.sems(tag, "v_done", "v_copied", "kv_loaded", "padded", "sigmoid_ready")
    rot_built, qk_done, qk_copied, rope_done = g.sems(tag, "rot_built", "qk_done", "qk_copied", "rope_done")
    scored, shift_ready, exp_done, p_turned, pt_copied, pv_done, o_ready = g.sems(
        tag, "scored", "shift_ready", "exp_done", "p_turned", "pt_copied", "pv_done", "o_ready")
    conv_ready, conv_sum, conv_centred, conv_squared, conv_var, conv_root, conv_scaled = g.sems(
        tag, "conv_ready", "conv_sum", "conv_centred", "conv_squared", "conv_var", "conv_root", "conv_scaled")
    head_loaded = [g.sem(f"head_loaded_{tag}{e}") for e in range(2)]
    with ExitStack() as s:
        sb = lambda n, shape: s.enter_context(nc.sbuf_tensor(f"{n}_{tag}", shape, F32))
        wkv = sb("w_ukv", [P, HEADS, NOPE + VD])
        wq_head = sb("w_uq_head", [P, 2, 2, QK])
        wq_rot = sb("w_uq_rot", [P, 2, 2, QK])
        wk_head = sb("w_uk_head", [P, 2, NOPE])
        v = sb("v", [P, NT, HEADS * VD])
        q_t = sb("q_t", [P, 2, W])
        rot = sb("q_rot", [P, SEQ])
        prob = sb("prob", [P, 2, TOK])
        prob_t = sb("prob_t", [P, 2, TOK])
        o = sb("o", [P, tiles, 2 * VD])
        soft = sb("soft", [P, 4, 2 * NT])
        z_a = sb("z_a", [P, 2, TOK + 3 * PAD_A])
        z_b = sb("z_b", [P, 2, TOK + 3 * PAD_B])
        acc_b = sb("acc_b", [P, 2, TOK + PAD_B])
        work = sb("work", [P, 3, TOK + PAD_B])
        rstd = sb("rstd", [P, 2, TOK])
        newton = sb("newton", [P, TOK])
        taps = list(range(1, 3))
        PER_PAIR = (CONV_B - 3) // (HEADS // 2)
        per_pair_tiles = 2 * tiles
        turned_per_pair = per_pair_tiles + 1

        def streams(pad):
            yield slice(0, SEQ), slice(pad, pad + SEQ)
            if not last_layer:
                yield slice(SEQ, TOK), slice(2 * pad + SEQ, 2 * pad + TOK)

        def key_range(u):
            return (0, TOK) if u < NX else (SEQ, TOK)

        with nc.Block() as block:
            @block.sync
            def _(sp):
                sp.dma_start(wkv[:], a["w_ukv"][l].rearrange("p (h n) -> p h n", h=HEADS)).then_inc(kv_loaded, 16)
                wq = a["w_uq"][l].rearrange("(k p) n -> p k n", p=P)
                wk = a["w_ukv"][l]
                with sp.Fori(0, HEADS // 2) as i:
                    for e in range(2):
                        sp.wait_ge(qk_done, i * 2 + (e + 1))
                        sp.dma_start(wq_head[:, e], wq[:, :, bass.ds(i * (2 * QK) + e * QK, QK)]).then_inc(head_loaded[e], 16)
                        sp.dma_start(wk_head[:, e], wk[:, bass.ds(i * (2 * P) + e * P, NOPE)]).then_inc(head_loaded[e], 16)

            @block.gpsimd
            def _(pool):
                pool.memset(z_a[:], 0.0).then_inc(padded, 1)
                pool.memset(z_b[:], 0.0).then_inc(padded, 1)
                pool.memset(wq_rot[:], 0.0).then_inc(padded, 1)

            @block.scalar
            def _(act):
                act.sem_inc(pt_copied, 1)
                act.sem_inc(exp_done, 1)
                act.activation(work[:, 0:2, 0:W], proj[:, QCHUNK:QCHUNK + 2, 0:W], ACT.Square).then_inc(latent_squared, 1)
                act.activation(work[:, 2, 0:TOK], proj[:, KVCHUNK], ACT.Square).then_inc(latent_squared, 1)
                for n, (i, w_) in enumerate(((0, W), (1, TOK))):
                    act.wait_ge(latent_mean, n + 1)
                    act.activation(rstd[:, i, 0:w_], work[:, i, 0:w_], ACT.Sqrt).then_inc(latent_root, 1)
                act.activation(proj[:, 8:10, 0:W], proj[:, 8:10, 0:W], ACT.Sigmoid).then_inc(sigmoid_ready, 1)
                for t in range(NT):
                    act.wait_ge(v_done, t + 1)
                    act.activation(v[:, t], g.ps[:, 4 + t % 2], ACT.Copy).then_inc(v_copied, 1)
                with act.Fori(0, HEADS // 2) as i:
                    for e in range(2):
                        act.wait_ge(qk_done, i * 2 + (e + 3))
                        act.activation(q_t[0:NOPE, e], g.psum2(0)[0:NOPE, 0:W], ACT.Copy).then_inc(qk_copied, 1)
                        if not last_layer:
                            act.activation(q_t[NOPE:QK, e, SEQ:], g.psum2(0)[NOPE:QK, SEQ:TOK], ACT.Copy).then_inc(qk_copied, 1)
                        act.activation(k_t[0:NOPE, e], g.psum2(1)[0:NOPE, 0:TOK], ACT.Copy).then_inc(qk_copied, 1)
                        for u in range(tiles):
                            lo, hi = key_range(u)
                            n = e * tiles + u
                            act.wait_ge(shift_ready, i * per_pair_tiles + (n + 1))
                            act.activation(prob[:, n % 2, lo:hi], g.psum2(n % 2)[:, lo:hi], ACT.Exp, scale=SCALE,
                                           bias=soft[:, 1, n:n + 1], accum_out=soft[:, 2, n:n + 1]).then_inc(exp_done, 1)
                            act.wait_ge(p_turned, i * turned_per_pair + (n + 1))
                            act.activation(prob_t[:, n % 2, lo:hi], g.psum2(2)[:, lo:hi], ACT.Copy).then_inc(pt_copied, 1)
                    act.wait_ge(p_turned, i * turned_per_pair + turned_per_pair)
                    act.activation(cat[:, bass.ds(i + 4, 1), 0:W].rearrange("p c n -> p (c n)"), g.psum2(2)[:, 0:W],
                                   ACT.Copy).then_inc(pt_copied, 1)
                act.wait_ge(conv_centred, 1)
                act.activation(work[:, 0:2, 0:W], acc_b[:, :, 0:W], ACT.Square).then_inc(conv_squared, 1)
                act.wait_ge(conv_var, 1)
                act.activation(rstd[:, 0, 0:W], work[:, 2, 0:W], ACT.Sqrt).then_inc(conv_root, 1)
                for c in range(2):
                    act.wait_ge(conv_scaled, c + 1)
                    act.activation(cat[:, 2 + c, 0:W], cat[:, 2 + c, 0:W], ACT.Silu, scale=g.cols[:, c, 35:36],
                                   bias=g.cols[:, c, 36:37])

            @block.vector
            def _(dve):
                link = Links(dve, g.dve_step)
                dve.wait_ge(latent_summed, 1)
                dve.tensor_scalar(work[:, 0, 0:W], g.psum2(0)[:, 0:W], 1.0 / (2 * P), EPS, ALU.mult, ALU.add).then_inc(latent_mean, 1)
                dve.wait_ge(latent_summed, 2)
                dve.tensor_scalar(work[:, 1, 0:TOK], g.psum2(1)[:, 0:TOK], 1.0 / P, EPS, ALU.mult, ALU.add).then_inc(latent_mean, 1)

                def refined_rstd(i, at, w_):
                    y, t, v_ = rstd[:, i, 0:w_], newton[:, 0:w_], work[:, at, 0:w_]
                    link(dve.reciprocal(y, y))
                    link(dve.tensor_tensor(t, y, y, ALU.mult))
                    link(dve.tensor_tensor(t, t, v_, ALU.mult))
                    link(dve.tensor_scalar(t, t, -0.5, 1.5, ALU.mult, ALU.add))
                    link(dve.tensor_tensor(y, y, t, ALU.mult))

                dve.wait_ge(latent_root, 1)
                refined_rstd(0, 0, W)
                for c in range(2):
                    dve.scalar_tensor_tensor(proj[:, QCHUNK + c, 0:W], proj[:, QCHUNK + c, 0:W], g.cols[:, c, 37:38],
                                             rstd[:, 0, 0:W], ALU.mult, ALU.mult).then_inc(latent_ready, 1)
                dve.wait_ge(latent_root, 2)
                refined_rstd(1, 1, TOK)
                dve.scalar_tensor_tensor(proj[:, KVCHUNK], proj[:, KVCHUNK], g.kvg[:, 0:1], rstd[:, 1], ALU.mult,
                                         ALU.mult).then_inc(latent_ready, 1)
                dve.wait_ge(padded, 3)
                dve.wait_ge(sigmoid_ready, 1)
                for tok, at in streams(PAD_A):
                    link.mark(dve.tensor_tensor(z_a[:, :, at], proj[:, 2:4, tok], proj[:, 4:6, tok], ALU.mult))
                for tok, at in streams(PAD_B):
                    link.mark(dve.tensor_tensor(z_b[:, :, at], proj[:, 6:8, tok], proj[:, 8:10, tok], ALU.mult))
                link.wait()
                acc_a = work[:, 1:3, 0:WA]
                for c in range(2):
                    link.mark(dve.tensor_scalar(acc_a[:, c], z_a[:, c, 0:WA], g.cols[:, c, 0:1], None, ALU.mult))
                for k in range(1, CONV_A):
                    for c in range(2):
                        link.wait(1)
                        link.mark(dve.scalar_tensor_tensor(acc_a[:, c], z_a[:, c, k:k + WA], g.cols[:, c, k:k + 1],
                                                           acc_a[:, c], ALU.mult, ALU.add))
                link.wait()
                for tok, at in streams(PAD_A):
                    out_at = slice(at.start - PAD_A, at.stop - PAD_A)
                    link.mark(dve.tensor_tensor(cat[:, 0:2, tok], proj[:, 0:2, tok], acc_a[:, :, out_at], ALU.mult))

                def tap(k, c):
                    link.wait(1)
                    at = bass.ds(k, WB)
                    w_at = bass.ds(k + CONV_A, 1)
                    link.mark(dve.scalar_tensor_tensor(acc_b[:, c, 0:WB], z_b[:, c, at], g.cols[:, c, w_at],
                                                       acc_b[:, c, 0:WB], ALU.mult, ALU.add))

                for c in range(2):
                    link.mark(dve.tensor_scalar(acc_b[:, c, 0:WB], z_b[:, c, 0:WB], g.cols[:, c, CONV_A:CONV_A + 1],
                                                g.cols[:, c, 34:35], ALU.mult, ALU.add))
                for k in taps:
                    for c in range(2):
                        tap(k, c)
                link.reset()
                rp = slice(NOPE, QK)
                with dve.Fori(0, HEADS // 2) as i:
                    todo = [(k, c) for k in range(PER_PAIR) for c in range(2)]
                    total = len(todo)

                    def o_part(n):
                        e, u = divmod(n, tiles)
                        dve.wait_ge(pv_done, i * per_pair_tiles + (n + 1))
                        link(dve.reciprocal(soft[:, 3, n:n + 1], soft[:, 2, n:n + 1]))
                        dve.tensor_scalar(o[:, u, e * VD:(e + 1) * VD], g.ps[:, 6 + n % 2, 0:VD],
                                          soft[:, 3, n:n + 1], None, ALU.mult).then_inc(o_ready, 1)

                    for e in range(2):
                        dve.wait_ge(head_loaded[e], i * 32 + 32)
                        src = wq_head[:, e, :, NOPE:QK].rearrange("p k (s u e) -> p k s u e", s=2, u=2)
                        dst = wq_rot[:, e, :, NOPE:QK].rearrange("p k (s u e) -> p k s u e", s=2, u=2)
                        dve.tensor_scalar(dst[:, :, :, 0], src[:, :, :, 1], -1.0, None, ALU.mult).then_inc(rot_built, 1)
                        dve.tensor_copy(dst[:, :, :, 1], src[:, :, :, 0]).then_inc(rot_built, 1)
                        dve.wait_ge(qk_done, i * 2 + (e + 3))
                        link.mark(dve.tensor_tensor(rot[rp], g.psum2(2)[rp, 0:SEQ], g.rope[rp, 1], ALU.mult))
                        link(dve.tensor_tensor(q_t[rp, e, 0:SEQ], g.psum2(0)[rp, 0:SEQ], g.rope[rp, 0], ALU.mult))
                        dve.tensor_tensor(q_t[rp, e, 0:SEQ], q_t[rp, e, 0:SEQ], rot[rp], ALU.add).then_inc(rope_done, 1)
                        for u in range(tiles):
                            lo, hi = key_range(u)
                            n = e * tiles + u
                            dve.wait_ge(scored, i * per_pair_tiles + (n + 1))
                            link(dve.tensor_reduce(soft[:, 0, n:n + 1], g.psum2(n % 2)[:, lo:hi], AX_X, ALU.max))
                            dve.tensor_scalar(soft[:, 1, n:n + 1], soft[:, 0, n:n + 1], -SCALE, None, ALU.mult
                                              ).then_inc(shift_ready, 1)
                            while total - len(todo) < (n + 1) * total // per_pair_tiles:
                                k, c = todo.pop(0)
                                tap(i * PER_PAIR + (3 + k), c)
                            if u >= 2:
                                o_part(n - 2)
                        o_part(n - 1)
                        o_part(n)
                    link.reset()
                dve.tensor_copy(acc_b[:, 0, 0:1], acc_b[:, 0, 0:1]).then_inc(conv_ready, 1)
                dve.wait_ge(conv_sum, 1)
                link(dve.tensor_scalar(work[:, 2, 0:W], g.psum2(0)[:, 0:W], 1.0 / (2 * P), None, ALU.mult))
                for c in range(2):
                    for tok, at in streams(PAD_B):
                        out_at = slice(at.start - PAD_B, at.stop - PAD_B)
                        link(dve.tensor_tensor(cat[:, 2 + c, tok], acc_b[:, c, out_at], work[:, 2, tok], ALU.subtract))
                dve.tensor_copy(acc_b[:, :, 0:W], cat[:, 2:4, 0:W]).then_inc(conv_centred, 1)
                dve.wait_ge(conv_sum, 2)
                dve.tensor_scalar(work[:, 2, 0:W], g.psum2(1)[:, 0:W], 1.0 / (2 * P), EPS, ALU.mult, ALU.add).then_inc(conv_var, 1)
                dve.wait_ge(conv_root, 1)
                refined_rstd(0, 2, W)
                for c in range(2):
                    dve.tensor_tensor(cat[:, 2 + c, 0:W], cat[:, 2 + c, 0:W], rstd[:, 0, 0:W], ALU.mult).then_inc(conv_scaled, 1)
                link.reset()

            @block.tensor
            def _(pe):
                def spans(n_tok):
                    return [(at, min(at + 512, n_tok)) for at in range(0, n_tok, 512)]

                pe.sem_inc(qk_done, 2)
                pe.wait_ge(latent_squared, 1)
                for c in range(2):
                    for lo, hi in spans(W):
                        last = pe.matmul(g.psum2(0)[:, lo:hi], g.ones[:], work[:, c, lo:hi], start=(c == 0), stop=(c == 1))
                last.then_inc(latent_summed, 1)
                pe.wait_ge(latent_squared, 2)
                for lo, hi in spans(TOK):
                    last = pe.matmul(g.psum2(1)[:, lo:hi], g.ones[:], work[:, 2, lo:hi], start=True, stop=True)
                last.then_inc(latent_summed, 1)
                pe.wait_ge(latent_ready, 3)
                pe.wait_ge(kv_loaded, 16)
                for t in range(NT):
                    if t >= 2:
                        pe.wait_ge(v_copied, t - 1)
                    pe.matmul(g.ps[:, 4 + t % 2], proj[:, KVCHUNK, t * P:(t + 1) * P], wkv[:, :, NOPE:],
                              start=True, stop=True).then_inc(v_done, 1)
                pe.wait_ge(v_copied, NT)
                with pe.Fori(0, HEADS // 2) as i:
                    copies = 2 if last_layer else 3
                    for e in range(2):
                        n0 = e * tiles
                        pe.wait_ge(head_loaded[e], i * 32 + 32)
                        pe.wait_ge(rot_built, i * 4 + (2 * e + 2))
                        pe.wait_ge(exp_done, i * per_pair_tiles + (n0 + 1))
                        pe.wait_ge(pt_copied, i * turned_per_pair + (n0 + 1))
                        for k in range(2):
                            for lo, hi in spans(W):
                                pe.matmul(g.psum2(0)[0:QK, lo:hi], wq_head[:, e, k, :], proj[:, QCHUNK + k, lo:hi],
                                          start=(k == 0), stop=(k == 1))
                            pe.matmul(g.psum2(2)[0:QK, 0:SEQ], wq_rot[:, e, k, :], proj[:, QCHUNK + k, 0:SEQ],
                                      start=(k == 0), stop=(k == 1))
                        for lo, hi in spans(TOK):
                            last = pe.matmul(g.psum2(1)[0:NOPE, lo:hi], wk_head[:, e, :], proj[:, KVCHUNK, lo:hi],
                                             start=True, stop=True)
                        last.then_inc(qk_done, 1)
                        pe.wait_ge(qk_copied, i * (2 * copies) + copies * (e + 1))
                        pe.wait_ge(rope_done, i * 2 + (e + 1))

                        def score(u):
                            n = n0 + u
                            if u >= 2:
                                pe.wait_ge(exp_done, i * per_pair_tiles + n)
                            lo, hi = key_range(u)
                            for at in range(lo, hi, 512):
                                to = min(at + 512, hi)
                                last = pe.matmul(g.psum2(n % 2)[:, at:to], q_t[0:QK, e, u * P:(u + 1) * P],
                                                 k_t[0:QK, e, at:to], start=True, stop=True)
                            last.then_inc(scored, 1)

                        def turn(u):
                            n = n0 + u
                            lo, hi = key_range(u)
                            pe.wait_ge(exp_done, i * per_pair_tiles + (n + 2))
                            pe.wait_ge(pt_copied, i * turned_per_pair + (n + 1))
                            for at in range(lo, hi, P):
                                last = pe.transpose(g.psum2(2)[:, at:at + P], prob[:, n % 2, at:at + P], g.ident[:])
                            last.then_inc(p_turned, 1)

                        def weigh(u):
                            n = n0 + u
                            lo, hi = key_range(u)
                            pe.wait_ge(pt_copied, i * turned_per_pair + (n + 2))
                            if n >= 2:
                                pe.wait_ge(o_ready, i * per_pair_tiles + (n - 1))
                            for at in range(lo, hi, P):
                                last = pe.matmul(g.ps[:, 6 + n % 2, 0:VD], prob_t[:, n % 2, at:at + P],
                                                 v[:, at // P, bass.ds(i * (2 * VD) + e * VD, VD)],
                                                 start=(at == lo), stop=(at + P == hi))
                            last.then_inc(pv_done, 1)

                        score(0)
                        for u in range(tiles):
                            if u + 1 < tiles:
                                score(u + 1)
                            if u >= 1:
                                weigh(u - 1)
                            turn(u)
                        weigh(tiles - 1)
                    pe.wait_ge(o_ready, i * per_pair_tiles + per_pair_tiles)
                    for u in range(tiles):
                        last = pe.transpose(g.psum2(2)[:, u * P:(u + 1) * P], o[:, u, :], g.ident[:])
                    last.then_inc(p_turned, 1)
                pe.wait_ge(conv_ready, 1)
                for c in range(2):
                    for tok, at in streams(PAD_B):
                        out_at = slice(at.start - PAD_B, at.stop - PAD_B)
                        last = pe.matmul(g.psum2(0)[:, tok], g.ones[:], acc_b[:, c, out_at], start=(c == 0), stop=(c == 1))
                last.then_inc(conv_sum, 1)
                pe.wait_ge(conv_squared, 1)
                for c in range(2):
                    for lo, hi in spans(W):
                        last = pe.matmul(g.psum2(1)[:, lo:hi], g.ones[:], work[:, c, lo:hi], start=(c == 0), stop=(c == 1))
                last.then_inc(conv_sum, 1)


@phase
def project_out(g, l, cat):
    nc, a = g.nc, g.a
    tiles = NX if l == DEPTH - 1 else NT
    w_loaded, tile_done, tile_scaled, = g.sems(f"{l}o", "w_loaded", "tile_done", "tile_scaled")
    with ExitStack() as s:
        w = s.enter_context(nc.sbuf_tensor(f"w_out_{l}", [P, KD, D], F32))
        with nc.Block() as block:
            @block.sync
            def _(sp):
                sp.dma_start(w[:], a["w_out"][l].rearrange("(k p) n -> p k n", p=P)).then_inc(w_loaded, 16)

            @block.tensor
            def _(pe):
                pe.wait_ge(w_loaded, 16)
                for t in range(tiles):
                    if t >= 2:
                        pe.wait_ge(tile_scaled, t - 1)
                    for k in range(KD):
                        for b in range(2):
                            last = pe.matmul(g.psum2(t % 2)[:, b * 512:(b + 1) * 512], cat[:, k, t * P:(t + 1) * P],
                                             w[:, k, b * 512:(b + 1) * 512], start=(k == 0), stop=(k == KD - 1))
                    last.then_inc(tile_done, 1)

            @block.vector
            def _(dve):
                link = Links(dve, g.dve_step)
                for t in range(tiles):
                    st = 0 if t < NX else 1
                    dve.wait_ge(tile_done, t + 1)
                    dve.tensor_tensor(g.rows[:, 0, 0], g.psum2(t % 2), g.rows[:, st, 2], ALU.mult).then_inc(tile_scaled, 1)
                    dve.wait_ge(tile_scaled, t + 1)
                    link(dve.tensor_tensor(g.x[:, t + 1], g.x[:, t + 1], g.rows[:, 0, 0], ALU.add))
                link.reset()


@phase
def peer(g, l, tiles, h, q_t, keys_t):
    nc, a = g.nc, g.a
    tag = f"{l}p"
    groups = tiles * PH
    blocks = groups // BLOCK
    (staged, scored, ranked, idx_ready, best_ready, gate_ready, dotted, acted, weighted, diag_ready, v_used,
     updated) = g.sems(tag, "staged", "scored", "ranked", "idx_ready", "best_ready", "gate_ready", "dotted",
                       "acted", "weighted", "diag_ready", "v_used", "updated")
    u_loaded = [g.sem(f"u_loaded_{tag}{n}") for n in range(NU)]
    v_loaded = [g.sem(f"v_loaded_{tag}{n}") for n in range(NV)]
    NDIAG = 4
    with ExitStack() as s:
        sb = lambda n, shape, dt=F32: s.enter_context(nc.sbuf_tensor(f"{n}_{tag}", shape, dt))
        u_buf = sb("u_rows", [P, NU, D])
        v_buf = sb("v_rows", [P, NV - 2, D])
        v_at = [v_buf[:, n] for n in range(NV - 2)] + [g.rows[:, 1, 0], g.rows[:, 1, 1]]
        h_tile, scaled = g.rows[:, 0, 0], g.rows[:, 0, 1]
        q_stage = sb("q_stage", [P, 2, 2, P])
        left = sb("left", [P, 2, P])
        top = sb("top", [P, 2, TOPK])
        top_i = sb("top_i", [P, 2, TOPK], U32)
        top_f = sb("top_f", [P, 2, TOPK])
        cand = sb("cand", [P, 2, TOPK * TOPK])
        best = sb("best", [P, 2, TOPK])
        best_i = sb("best_i", [P, TOPK], U32)
        pair_i = sb("pair_i", [P, 2, TOPK], U32)
        pair_f = sb("pair_f", [P, 2, TOPK])
        match = sb("match", [P, 2, TOPK, TOPK])
        found = sb("found", [P, 2, TOPK])
        shift = sb("shift", [P, 2, 1])
        total = sb("total", [P, 2, 2])
        idx = sb("idx", [P, BLOCK, TOPK], U32)
        gate = sb("gate", [P, 2, TOPK])
        dots = sb("dots", [P, 2, TOPK])
        gelu = sb("gelu", [P, 2, TOPK])
        wts = sb("wts", [P, 2, TOPK])
        diag = sb("diag", [P, NDIAG, P])

        def at_group(b, k):
            return b + k // BLOCK, k % BLOCK

        def exists(b, k):
            return not isinstance(b, int) or b * BLOCK + k < groups

        def each_block(eng, body):
            with eng.Fori(0, blocks - 1) as b:
                body(b)
            body(blocks - 1)

        with nc.Block() as block:
            @block.gpsimd
            def _(pool):
                def gather(buf, table, k, j, loaded):
                    pool.nop(nofuse=True)
                    pool.indirect_dma_start(buf, None, table.rearrange("l e d -> (l e) d"),
                                            bass.IndirectOffsetOnAxis(idx[:, k % BLOCK, j:j + 1], 0),
                                            element_offset=l * NKEY * NKEY * D).then_inc(loaded, 16)

                pool.wait_ge(idx_ready, 1)
                for j in range(TOPK):
                    if j >= NU:
                        pool.wait_ge(dotted, j - NU + 1)
                    gather(u_buf[:, j % NU], a["peer_u"], 0, j, u_loaded[j % NU])

                def body(b):
                    for k in range(BLOCK):
                        with_u = exists(b, k + 1)
                        if with_u:
                            pool.wait_ge(idx_ready, b * BLOCK + (k + 2))
                        for j in range(TOPK):
                            if with_u:
                                pool.wait_ge(dotted, b * (BLOCK * TOPK) + ((k + 1) * TOPK + j - NU + 1))
                                gather(u_buf[:, j % NU], a["peer_u"], k + 1, j, u_loaded[j % NU])
                            pool.wait_ge(v_used, b * (BLOCK * TOPK) + (k * TOPK + j + 1))
                            gather(v_at[j % NV], a["peer_v"], k, j, v_loaded[j % NV])

                each_block(pool, body)

            @block.scalar
            def _(act):
                def stage(b, k):
                    if not exists(b, k):
                        return
                    bb, kk = at_group(b, k)
                    if not (isinstance(b, int) and b * BLOCK + k < 2):
                        act.wait_ge(scored, b * BLOCK + (k - 1))
                    act.activation(q_stage[:, k % 2], q_t[:, bass.ds((bb % 2) * (2 * BLOCK) + 2 * kk, 2),
                                                          bass.ds((bb // 2) * P, P)], ACT.Copy).then_inc(staged, 1)

                def gates(b, k):
                    if not exists(b, k):
                        return
                    act.wait_ge(best_ready, b * BLOCK + (k + 1))
                    act.activation(gate[:, k % 2], best[:, k % 2], ACT.Exp, bias=shift[:, k % 2],
                                   accum_out=total[:, k % 2, 0:1]).then_inc(gate_ready, 1)

                stage(0, 0)
                stage(0, 1)
                gates(0, 0)

                def body(b):
                    for k in range(BLOCK):
                        stage(b, k + 2)
                        gates(b, k + 1)
                        act.wait_ge(dotted, b * (BLOCK * TOPK) + (k + 1) * TOPK)
                        act.activation(gelu[:, k % 2], dots[:, k % 2], ACT.Gelu).then_inc(acted, 1)
                        act.wait_ge(weighted, b * BLOCK + (k + 1))
                        for j in range(TOPK):
                            act.wait_ge(v_used, b * (BLOCK * TOPK) + (k * TOPK + j + 1 - NDIAG + NV))
                            act.activation(diag[:, j % NDIAG], g.ident[:], ACT.Copy, scale=wts[:, k % 2, j:j + 1]
                                           ).then_inc(diag_ready, 1)

                each_block(act, body)

            @block.vector
            def _(dve):
                link = Links(dve, g.dve_step)

                def route(b, k):
                    if not exists(b, k):
                        return
                    r = k % 2
                    dve.wait_ge(scored, b * BLOCK + (k + 1))
                    dve.nop(nofuse=True)
                    for p in range(2):
                        sc = g.ps[:, r, p * P:(p + 1) * P]
                        link(dve.max(top[:, p, 0:8], sc))
                        link.mark(dve.max_index(top_i[:, p, 0:8], top[:, p, 0:8], sc))
                        link(dve.match_replace(left[:, p], top[:, p, 0:8], sc, LOWEST))
                        link(dve.max(top[:, p, 8:16], left[:, p]))
                        dve.max_index(top_i[:, p, 8:16], top[:, p, 8:16], left[:, p]).then_inc(ranked, 1)
                    dve.wait_ge(ranked, b * (2 * BLOCK) + (2 * k + 2))
                    link.mark(dve.tensor_tensor(cand[:, 0].rearrange("p (i j) -> p i j", i=TOPK),
                                                top[:, 0].unsqueeze(2).broadcast_to([P, TOPK, TOPK]),
                                                top[:, 1].unsqueeze(1).broadcast_to([P, TOPK, TOPK]), ALU.add))
                    link(dve.tensor_copy(top_f[:], top_i[:]))
                    link(dve.max(best[:, r, 0:8], cand[:, 0]))
                    link.mark(dve.max_index(best_i[:, 0:8], best[:, r, 0:8], cand[:, 0]))
                    link(dve.match_replace(cand[:, 1], best[:, r, 0:8], cand[:, 0], LOWEST))
                    link(dve.max(best[:, r, 8:16], cand[:, 1]))
                    link.mark(dve.max_index(best_i[:, 8:16], best[:, r, 8:16], cand[:, 1]))
                    dve.tensor_scalar(shift[:, r], best[:, r, 0:1], -1.0, None, ALU.mult).then_inc(best_ready, 1)
                    link.wait()
                    link.mark(dve.tensor_scalar(pair_i[:, 0], best_i[:], 4, None, ALU.logical_shift_right))
                    link(dve.tensor_scalar(pair_i[:, 1], best_i[:], TOPK - 1, None, ALU.bitwise_and))
                    link(dve.tensor_copy(pair_f[:], pair_i[:]))
                    for p in range(2):
                        link.mark(dve.tensor_tensor(match[:, p], pair_f[:, p].unsqueeze(2).broadcast_to([P, TOPK, TOPK]),
                                                    g.iota[:].unsqueeze(1).broadcast_to([P, TOPK, TOPK]), ALU.is_equal))
                    for p in range(2):
                        link.wait(1)
                        link.mark(dve.tensor_tensor(match[:, p], match[:, p],
                                                    top_f[:, p].unsqueeze(1).broadcast_to([P, TOPK, TOPK]), ALU.mult))
                    link.wait()
                    link(dve.tensor_reduce(found[:], match[:], AX_X, ALU.add))
                    dve.scalar_tensor_tensor(idx[:, k % BLOCK], found[:, 0], float(NKEY), found[:, 1], ALU.mult, ALU.add
                                             ).then_inc(idx_ready, 1)

                def update():
                    pass

                route(0, 0)
                link.reset()

                def body(b):
                    link(dve.tensor_copy(h_tile, h[:, bass.ds(b // 2, 1)].rearrange("p t d -> p (t d)")))
                    for k in range(BLOCK):
                        r = k % 2
                        route(b, k + 1)
                        for j in range(TOPK):
                            dve.wait_ge(u_loaded[j % NU], b * (16 * BLOCK * TOPK // NU) + 16 * ((k * TOPK + j) // NU + 1))
                            dve.tensor_tensor_reduce(u_buf[:, j % NU], u_buf[:, j % NU], h_tile, 1.0, 0.0, ALU.mult,
                                                     ALU.add, dots[:, r, j:j + 1]).then_inc(dotted, 1)
                        dve.wait_ge(gate_ready, b * BLOCK + (k + 1))
                        link(dve.reciprocal(total[:, r, 1:2], total[:, r, 0:1]))
                        dve.wait_ge(acted, b * BLOCK + (k + 1))
                        dve.scalar_tensor_tensor(wts[:, r], gelu[:, r], total[:, r, 1:2], gate[:, r], ALU.mult, ALU.mult
                                                 ).then_inc(weighted, 1)
                        if k == 0:
                            half_update(b)
                    link.reset()

                def half_update(b):
                    t1 = (b + 1) // 2
                    dve.wait_ge(v_used, b * (BLOCK * TOPK) + NV)
                    link(dve.tensor_tensor(scaled, g.psum2(1), g.rows[:, bass.ds((t1 + 3) // 8, 1), 2].rearrange(
                        "p s n -> p (s n)"), ALU.mult))
                    xt = g.x[:, bass.ds(t1, 1)].rearrange("p t n -> p (t n)")
                    dve.tensor_tensor(xt, xt, scaled, ALU.add).then_inc(updated, 1)

                link(dve.memset(g.psum2(1), 0.0))
                link.reset()
                each_block(dve, body)
                half_update(blocks)
                link.reset()

            @block.tensor
            def _(pe):
                pe.sem_inc(v_used, NV)

                def scores(b, k):
                    if not exists(b, k):
                        return
                    bb, kk = at_group(b, k)
                    pe.wait_ge(staged, b * BLOCK + (k + 1))
                    if not (isinstance(b, int) and b * BLOCK + k < 2):
                        pe.wait_ge(ranked, b * (2 * BLOCK) + 2 * (k - 1))
                    for p in range(2):
                        last = pe.matmul(g.ps[:, k % 2, p * P:(p + 1) * P], q_stage[:, k % 2, p],
                                         keys_t[:, bass.ds((bb % 2) * (2 * BLOCK) + (2 * kk + p), 1)].rearrange(
                                             "p c n -> p (c n)"), start=True, stop=True)
                    last.then_inc(scored, 1)

                scores(0, 0)
                scores(0, 1)

                def body(b):
                    for k in range(BLOCK):
                        scores(b, k + 2)
                        if k == 0:
                            pe.wait_ge(updated, b + 1)
                        for j in range(TOPK):
                            f = k * TOPK + j
                            pe.wait_ge(v_loaded[j % NV], b * (16 * BLOCK * TOPK // NV) + 16 * (f // NV + 1))
                            pe.wait_ge(diag_ready, b * (BLOCK * TOPK) + (f + 1))
                            for c in range(2):
                                last = pe.matmul(g.psum2(1)[:, c * 512:(c + 1) * 512], diag[:, j % NDIAG],
                                                 v_at[j % NV][:, c * 512:(c + 1) * 512], start=(f == 0),
                                                 stop=(f == BLOCK * TOPK - 1))
                            last.then_inc(v_used, 1)

                each_block(pe, body)


@phase
def final_norm(g):
    nc, a = g.nc, g.a
    row_loaded, squared, mean_ready, rstd_ready, tile_ready, stored = g.sems(
        "f", "row_loaded", "squared", "mean_ready", "rstd_ready", "tile_ready", "stored")
    with ExitStack() as s:
        sb = lambda n, shape: s.enter_context(nc.sbuf_tensor(n, shape, F32))
        grow, y, stat = sb("final_row", [P, D]), sb("final", [P, NX, D]), sb("final_stat", [P, 3, NX])
        with nc.Block() as block:
            @block.sync
            def _(sp):
                sp.dma_start(grow[:], a["final_norm_g"].partition_broadcast(P)).then_inc(row_loaded, 16)
                for t in range(NX):
                    sp.wait_ge(tile_ready, t + 1)
                    sp.dma_start(a["out"][0, t * P:(t + 1) * P, :], y[:, t]).then_inc(stored, 16)
                sp.wait_ge(stored, 16 * NX)

            @block.scalar
            def _(act):
                for t in range(NX):
                    act.activation(y[:, t], g.x[:, t + 1], ACT.Square, accum_out=stat[:, 0, t:t + 1]).then_inc(squared, 1)

            @block.gpsimd
            def _(pool):
                pool.wait_ge(mean_ready, 1)
                pool.tensor_tensor(stat[:, 2], stat[:, 1], g.half[:, 0:NX], ALU.pow).then_inc(rstd_ready, 1)

            @block.vector
            def _(dve):
                dve.wait_ge(squared, NX)
                dve.tensor_scalar(stat[:, 1], stat[:, 0], 1.0 / D, EPS, ALU.mult, ALU.add).then_inc(mean_ready, 1)
                dve.wait_ge(rstd_ready, 1)
                dve.wait_ge(row_loaded, 16)
                for t in range(NX):
                    dve.scalar_tensor_tensor(y[:, t], g.x[:, t + 1], stat[:, 2, t:t + 1], grow[:], ALU.mult, ALU.mult
                                             ).then_inc(tile_ready, 1)


def trunk(nc, a):
    with ExitStack() as stack:
        g = Program(nc, stack, a)
        modulation(g)
        for l in range(DEPTH):
            last_layer = l == DEPTH - 1
            with ExitStack() as s:
                sb = lambda n, shape: s.enter_context(nc.sbuf_tensor(f"{n}_{l}", shape, F32))
                k_t = sb("k_t", [P, 2, TOK])
                cat = sb("cat", [P, KD, NX * P if last_layer else TOK])
                with ExitStack() as s2:
                    proj = s2.enter_context(nc.sbuf_tensor(f"proj_{l}", [P, NPROJ, TOK], F32))
                    with nc.sbuf_tensor(f"h1_{l}", [P, NT, D], F32) as h:
                        norm_and_project(g, l, 0, NT, h, {"proj": proj, "k_t": k_t})
                    mix(g, l, proj, k_t, cat)
                project_out(g, l, cat)
            tiles = NX if last_layer else NT
            with ExitStack() as s:
                sb = lambda n, shape: s.enter_context(nc.sbuf_tensor(f"{n}_{l}", shape, F32))
                h = sb("h2", [P, tiles, D])
                q_t = sb("peer_q_t", [P, 2 * PH, tiles * P])
                keys_t = sb("keys_t", [P, 2 * PH, P])
                norm_and_project(g, l, 1, tiles, h, {"proj": q_t, "keys_t": keys_t})
                peer(g, l, tiles, h, q_t, keys_t)
        final_norm(g)


_INS = ["x", "c", "ctx", "c_ctx", "w_mod", "b_mod", "norm1_g", "norm2_g", "w_in", "w_out", "conv_a_w", "conv_b_w",
        "conv_b_bias", "conv_b_ln_g", "conv_b_ln_b", "mla_q_norm_g", "w_uq", "mla_kv_norm_g", "w_ukv", "peer_w_q",
        "peer_sub_keys", "peer_u", "peer_v", "final_norm_g"]


def shape_constants():
    axis = ROPE // 2
    inv = (ROPE_BASE ** (-np.arange(0, axis, 2, dtype=np.float32) / axis)).astype(np.float32)
    n = np.arange(SEQ)
    ar = (n // GRID_W).astype(np.float32)[:, None] * inv
    ac = (n % GRID_W).astype(np.float32)[:, None] * inv
    ang = np.concatenate([ar, ar, ac, ac], axis=-1).T
    tables = np.stack([np.cos(ang), np.sin(ang)], axis=1).astype(np.float32)
    return {"identity": np.eye(P, dtype=np.float32), "rope_tables": np.ascontiguousarray(tables)}


def kernel(**inputs):
    import concourse.bacc as _bacc
    from concourse.bass_utils import run_bass_kernel_spmd as _run

    nc = _bacc.Bacc("TRN2", target_bir_lowering=False, num_devices=1)
    arrays, args = {}, {}
    host = {n: np.ascontiguousarray(inputs[n]) for n in _INS}
    host.update(shape_constants())
    for name, v in host.items():
        arrays[f"in_{name}"] = v
        args[name] = nc.dram_tensor(f"in_{name}", v.shape, mybir.dt.from_np(v.dtype), kind="ExternalInput").ap()
    args["out"] = nc.dram_tensor("out_0", (1, SEQ, D), F32, kind="ExternalOutput").ap()
    trunk(nc, args)
    r = _run(nc, [arrays], core_ids=[0])
    return r.results[0]["out_0"]
```

```python
from contextlib import ExitStack

import numpy as np

import concourse.bass as bass
from concourse import mybir

F32 = mybir.dt.float32
U32 = mybir.dt.uint32
ALU = mybir.AluOpType
ACT = mybir.ActivationFunctionType
AX_X = mybir.AxisListType.X

P = 128
D = 1024
KD = D // P
DEPTH = 2
SEQ, CTX = 512, 256
TOK = SEQ + CTX
NX, NT = SEQ // P, TOK // P
HEADS, NOPE, ROPE, VD = 8, 64, 32, 64
QK = NOPE + ROPE
SCALE = QK ** -0.5
CONV_A, CONV_B = 3, 31
PAD_A, PAD_B = CONV_A // 2, CONV_B // 2
QCHUNK, KVCHUNK, KRCHUNK = 10, 12, 13
NPROJ = 13
EPS = 1e-6
PH, NKEY, TOPK = 8, 128, 16
LOWEST = -3.0e38
NU = NV = 8
SLABS = 3
GRID_W, ROPE_BASE = 64, 10000.0


class Links:

    def __init__(self, eng, sem):
        self.eng, self.sem, self.n = eng, sem, 0

    def mark(self, ins):
        self.n += 1
        ins.then_inc(self.sem, 1)

    def wait(self, behind=0):
        if self.n > behind:
            self.eng.wait_ge(self.sem, self.n - behind)

    def __call__(self, ins):
        self.mark(ins)
        self.wait()

    def reset(self):
        self.wait()
        if self.n:
            self.eng.sem_clear(self.sem)
        self.n = 0


class Program:

    def __init__(self, nc, stack, a):
        self.nc, self.stack, self.a = nc, stack, a
        sb = self.sb
        self.x = sb("x_tiles", [P, NT, D])
        self.rows = sb("mod_rows", [P, 2, 3, D])
        self.ident = sb("ident", [P, P])
        self.ones = sb("ones", [P, P])
        self.rope = sb("rope", [P, 2, SEQ])
        self.half = sb("minus_half", [P, NT])
        self.iota = sb("iota16", [P, TOPK])
        self.cols = sb("cols", [P, 2, 38])
        self.kvg = sb("kv_norm_g", [P, 1])
        self.ps = stack.enter_context(nc.psum_tensor("psum", [P, 8, 512], F32))
        self.mod_dram = nc.dram_tensor("mod_dram", (2, DEPTH * 6 * D), F32, kind="Internal").ap()
        self.dve_step = stack.enter_context(nc.semaphore("dve_step"))

    def sb(self, name, shape, dt=F32):
        return self.stack.enter_context(self.nc.sbuf_tensor(name, shape, dt))

    def sem(self, name):
        self.phase_sems.append(self.sem_stack.enter_context(self.nc.semaphore(name)))
        return self.phase_sems[-1]

    def sems(self, tag, *names):
        return [self.sem(f"{n}_{tag}") for n in names]

    def psum2(self, b):
        return self.ps[:, 2 * b:2 * b + 2, :].rearrange("p b n -> p (b n)")


def phase(build):
    def run(g, *args):
        with ExitStack() as g.sem_stack:
            g.phase_sems = []
            build(g, *args)
            numbers = sorted(x.num for x in g.phase_sems)
            starts = [n for n in numbers if n - 1 not in numbers]
            ends = [n + 1 for n in numbers if n + 1 not in numbers]
            for first, end in zip(starts, ends):
                g.nc.gpsimd.sem_clear(range(first, end))
            g.nc.all_engine_barrier()
    return run


@phase
def modulation(g):
    nc, a = g.nc, g.a
    NCH = 6 * D // 512
    tensors_loaded, c_ready, row_done, row_added, rows_out = g.sems("m", "tensors_loaded", "c_ready", "row_done",
                                                                     "row_added", "rows_out")
    c_loaded, zeroed, bias_loaded = g.sems("m", "c_loaded", "zeroed", "bias_loaded")
    slab_loaded = [g.sem(f"slab_loaded_m{r}") for r in range(SLABS)]
    with ExitStack() as s:
        sb = lambda n, shape: s.enter_context(nc.sbuf_tensor(n, shape, F32))
        slab = sb("mod_slab", [P, SLABS, KD, 512])
        c = sb("c_cols", [P, KD, 2])
        e = sb("c_exp", [P, KD, 2])
        bias = sb("mod_bias", [2, DEPTH * 6 * D])
        rows = sb("mod_out", [2, DEPTH * 6 * D])
        with nc.Block() as block:
            @block.sync
            def _(sp):
                with nc.allow_non_contiguous_dma(reason="a vector onto partitions"):
                    sp.dma_start(c[:, :, 0], a["c"].rearrange("b (k p) -> p (b k)", p=P)).then_inc(c_loaded, 16)
                    sp.dma_start(c[:, :, 1], a["c_ctx"].rearrange("(k p) -> p k", p=P)).then_inc(c_loaded, 16)
                sp.dma_start(bias[:], a["b_mod"].rearrange("l n -> (l n)").partition_broadcast(2)).then_inc(bias_loaded, 16)
                for l in range(DEPTH):
                    w = a["w_mod"][l].rearrange("(k p) n -> p k n", p=P)
                    with sp.Fori(0, NCH // SLABS) as i:
                        for r in range(SLABS):
                            sp.wait_ge(row_done, i * SLABS + (l * NCH + r + 1))
                            sp.dma_start(slab[:, r], w[:, :, bass.ds(i * (SLABS * 512) + r * 512, 512)]
                                         ).then_inc(slab_loaded[r], 16)
                    if l == 0:
                        sp.dma_start(g.x[:, 0:NX], a["x"].rearrange("b (t p) d -> p (b t) d", p=P)
                                     ).then_inc(tensors_loaded, 16)
                        sp.dma_start(g.x[:, NX:], a["ctx"].rearrange("b (t p) d -> p (b t) d", p=P)
                                     ).then_inc(tensors_loaded, 16)
                        sp.dma_start(g.ident[:], a["identity"]).then_inc(tensors_loaded, 16)
                        sp.dma_start(g.rope[NOPE:QK], a["rope_tables"]).then_inc(tensors_loaded, 16)
                sp.wait_ge(row_added, DEPTH * NCH + SLABS)
                sp.dma_start(g.mod_dram, rows[:]).then_inc(rows_out, 16)
                sp.wait_ge(rows_out, 16)
                sp.wait_ge(tensors_loaded, 64)

            @block.gpsimd
            def _(pool):
                pool.memset(g.ones[:], 1.0)
                pool.memset(g.half[:], -0.5)
                pool.iota(g.iota[:], [[1, TOPK]], base=0, channel_multiplier=0,
                          allow_small_or_imprecise_dtypes=True)

            @block.scalar
            def _(act):
                act.wait_ge(c_loaded, 32)
                act.activation(e[:], c[:], ACT.Exp, scale=-1.0).then_inc(zeroed, 1)

            @block.vector
            def _(dve):
                link = Links(dve, g.dve_step)
                dve.sem_inc(row_added, SLABS)
                dve.wait_ge(zeroed, 1)
                link(dve.tensor_scalar(e[:], e[:], 1.0, None, ALU.add))
                link(dve.reciprocal(e[:], e[:]))
                dve.tensor_tensor(c[:], c[:], e[:], ALU.mult).then_inc(c_ready, 1)
                dve.wait_ge(bias_loaded, 16)
                for l in range(DEPTH):
                    with dve.Fori(0, NCH // SLABS) as i:
                        for r in range(SLABS):
                            at = bass.ds(i * (SLABS * 512) + (l * NCH + r) * 512, 512)
                            dve.wait_ge(row_done, i * SLABS + (l * NCH + r + 1 + SLABS))
                            dve.tensor_tensor(rows[:, at], g.ps[0:2, r, :], bias[:, at], ALU.add).then_inc(row_added, 1)
                link.reset()

            @block.tensor
            def _(pe):
                pe.sem_inc(row_done, SLABS)
                pe.wait_ge(c_ready, 1)
                for l in range(DEPTH):
                    with pe.Fori(0, NCH // SLABS) as i:
                        for r in range(SLABS):
                            pe.wait_ge(slab_loaded[r], i * 16 + 16 * (l * NCH // SLABS + 1))
                            pe.wait_ge(row_added, i * SLABS + (l * NCH + r + 1))
                            for k in range(KD):
                                last = pe.matmul(g.ps[0:2, r, :], c[:, k, :], slab[:, r, k, :],
                                                 start=(k == 0), stop=(k == KD - 1))
                            last.then_inc(row_done, 1)


def load_mod_rows(g, sp, l, which, loaded):
    at = (l * 6 + which * 3) * D
    for s in range(2):
        sp.dma_start(g.rows[:, s].rearrange("p r n -> p (r n)"),
                     g.mod_dram[s, at:at + 3 * D].partition_broadcast(P)).then_inc(loaded, 16)


@phase
def norm_and_project(g, l, which, tiles, h, out):
    nc, a = g.nc, g.a
    tag = f"{l}{which}"
    rows_loaded, squared, mean_ready, rstd_ready, h_ready, transposed, ht_ready, chunk_done, chunk_copied = g.sems(
        tag, "rows_loaded", "squared", "mean_ready", "rstd_ready", "h_ready", "transposed", "ht_ready",
        "chunk_done", "chunk_copied")
    rot_slab_ready, keys_loaded, rope_in, cols_loaded = g.sems(tag, "rot_slab_ready", "keys_loaded", "rope_in", "cols_loaded")
    slab_loaded = [g.sem(f"slab_loaded_{tag}{r}") for r in range(2)]
    if which == 0:
        w = a["w_in"][l].rearrange("(k p) n -> p k n", p=P)
    norm_g = (a["norm1_g"] if which == 0 else a["norm2_g"])[l]
    looped = 12 if which == 0 else 2
    tokens = tiles * P
    wide = SEQ if which == 0 and l == DEPTH - 1 else tokens
    with ExitStack() as s:
        sb = lambda n, shape: s.enter_context(nc.sbuf_tensor(f"{n}_{tag}", shape, F32))
        grow = sb("norm_g_row", [P, D])
        ht = out["h_t"]
        slab = sb("slab", [P, 2, KD, P])
        stat = sb("stat", [P, 3, NT])
        if which == 0:
            rot_slab = sb("rot_slab", [P, KD, QK])
            kr_raw = sb("kr_raw", [P, TOK])
            kr_rot = sb("kr_rot", [P, SEQ])

        def stream(t):
            return 0 if t < NX else 1

        with nc.Block() as block:
            @block.sync
            def _(sp):
                load_mod_rows(g, sp, l, which, rows_loaded)
                sp.dma_start(grow[:], norm_g.partition_broadcast(P)).then_inc(rows_loaded, 16)
                if which == 1:
                    for r in range(2):
                        sp.dma_start(slab[:, r], a["peer_w_q"][l, r]).then_inc(slab_loaded[r], 16)
                    sp.dma_start(out["keys_t"][:], a["peer_sub_keys"][l]).then_inc(keys_loaded, 16)
                    sp.wait_ge(keys_loaded, 16)
                else:
                    with sp.Fori(0, looped // 2) as i:
                        for r in range(2):
                            sp.wait_ge(chunk_done, i * 2 + (r + 1))
                            sp.dma_start(slab[:, r], w[:, :, bass.ds(i * (2 * P) + r * P, P)]).then_inc(slab_loaded[r], 16)
                    sp.wait_ge(chunk_done, looped + 1)
                    sp.dma_start(slab[:, 0], w[:, :, KVCHUNK * P:(KVCHUNK + 1) * P]).then_inc(slab_loaded[0], 16)
                    sp.wait_ge(chunk_done, looped + 2)
                    sp.dma_start(slab[:, 1, :, 0:QK], w[:, :, KRCHUNK * P - NOPE:]).then_inc(slab_loaded[1], 16)
                    with nc.allow_non_contiguous_dma(reason="vectors onto partitions"):
                        col = lambda name: a[name][l].rearrange("(c p) -> p c", p=P)
                        sp.dma_start(g.cols[:, :, 34], col("conv_b_bias")).then_inc(cols_loaded, 16)
                        sp.dma_start(g.cols[:, :, 35], col("conv_b_ln_g")).then_inc(cols_loaded, 16)
                        sp.dma_start(g.cols[:, :, 36], col("conv_b_ln_b")).then_inc(cols_loaded, 16)
                        sp.dma_start(g.cols[:, :, 37], col("mla_q_norm_g")).then_inc(cols_loaded, 16)
                        sp.dma_start(g.kvg[:], col("mla_kv_norm_g")).then_inc(cols_loaded, 16)
                        for c in range(2):
                            sp.dma_start(g.cols[:, c, 0:CONV_A], a["conv_a_w"][l][:, c * P:(c + 1) * P].rearrange(
                                "k p -> p k")).then_inc(cols_loaded, 16)
                            sp.dma_start(g.cols[:, c, CONV_A:CONV_A + CONV_B], a["conv_b_w"][l][:, c * P:(c + 1) * P].rearrange(
                                "k p -> p k")).then_inc(cols_loaded, 16)
                    sp.wait_ge(cols_loaded, 16 * 9)

            @block.scalar
            def _(act):
                act.sem_inc(chunk_copied, 2)
                for t in range(tiles):
                    act.activation(h[:, t], g.x[:, t], ACT.Square, accum_out=stat[:, 0, t:t + 1]).then_inc(squared, 1)
                for t in range(tiles):
                    act.wait_ge(transposed, t + 1)
                    act.activation(ht[:, :, t * P:(t + 1) * P], g.psum2(t % 2).rearrange("p (k n) -> p k n", k=KD),
                                   ACT.Copy).then_inc(ht_ready, 1)
                with act.Fori(0, looped // 2) as i:
                    for r in range(2):
                        act.wait_ge(chunk_done, i * 2 + (r + 3))
                        act.activation(out["proj"][:, bass.ds(i * 2 + r, 1), 0:wide].rearrange("p c n -> p (c n)"),
                                       g.psum2(r)[:, 0:wide], ACT.Copy).then_inc(chunk_copied, 1)
                if which == 0:
                    act.wait_ge(chunk_done, looped + 3)
                    act.activation(out["proj"][:, KVCHUNK], g.psum2(0)[:, 0:TOK], ACT.Copy).then_inc(chunk_copied, 1)
                    act.wait_ge(chunk_done, looped + 4)
                    act.activation(kr_raw[NOPE:QK], g.psum2(1)[NOPE:QK, 0:TOK], ACT.Copy).then_inc(rope_in, 1)
                    act.wait_ge(chunk_done, looped + 5)
                    act.activation(kr_rot[NOPE:QK], g.psum2(2)[NOPE:QK, 0:SEQ], ACT.Copy).then_inc(rope_in, 1)

            @block.gpsimd
            def _(pool):
                pool.wait_ge(mean_ready, 1)
                pool.tensor_tensor(stat[:, 2, 0:tiles], stat[:, 1, 0:tiles], g.half[:, 0:tiles], ALU.pow).then_inc(rstd_ready, 1)
                if which == 0:
                    pool.memset(rot_slab[:], 0.0).then_inc(rot_slab_ready, 1)

            @block.vector
            def _(dve):
                link = Links(dve, g.dve_step)
                dve.wait_ge(rows_loaded, 48)
                for st in range(2):
                    link(dve.scalar_tensor_tensor(g.rows[:, st, 1], g.rows[:, st, 1], 1.0, grow[:], ALU.add, ALU.mult))
                dve.wait_ge(squared, tiles)
                dve.tensor_scalar(stat[:, 1, 0:tiles], stat[:, 0, 0:tiles], 1.0 / D, EPS, ALU.mult, ALU.add
                                  ).then_inc(mean_ready, 1)
                dve.wait_ge(rstd_ready, 1)
                for t in range(tiles):
                    link(dve.scalar_tensor_tensor(h[:, t], g.x[:, t], stat[:, 2, t:t + 1], g.rows[:, stream(t), 1],
                                                  ALU.mult, ALU.mult))
                    dve.tensor_tensor(h[:, t], h[:, t], g.rows[:, stream(t), 0], ALU.add).then_inc(h_ready, 1)
                if which == 0:
                    dve.wait_ge(rot_slab_ready, 1)
                    dve.wait_ge(slab_loaded[1], 16 * (looped // 2 + 1))
                    src = slab[:, 1, :, NOPE:QK].rearrange("p k (s u e) -> p k s u e", s=2, u=2)
                    dst = rot_slab[:, :, NOPE:QK].rearrange("p k (s u e) -> p k s u e", s=2, u=2)
                    link.mark(dve.tensor_scalar(dst[:, :, :, 0], src[:, :, :, 1], -1.0, None, ALU.mult))
                    dve.tensor_copy(dst[:, :, :, 1], src[:, :, :, 0]).then_inc(rot_slab_ready, 1)
                    link.wait()
                    dve.wait_ge(rope_in, 2)
                    kr = slice(NOPE, QK)
                    link(dve.tensor_tensor(kr_rot[kr], kr_rot[kr], g.rope[kr, 1], ALU.mult))
                    for e in range(2):
                        kt = out["k_t"]
                        link.mark(dve.tensor_copy(kt[kr, e, SEQ:], kr_raw[kr, SEQ:]))
                        link(dve.tensor_tensor(kt[kr, e, 0:SEQ], kr_raw[kr, 0:SEQ], g.rope[kr, 0], ALU.mult))
                        link(dve.tensor_tensor(kt[kr, e, 0:SEQ], kt[kr, e, 0:SEQ], kr_rot[kr], ALU.add))
                link.reset()

            @block.tensor
            def _(pe):
                pe.sem_inc(chunk_done, 2)

                def chunk(psum, lhs, m, n_tok):
                    for k in range(KD):
                        for at in range(0, n_tok, 512):
                            to = min(at + 512, n_tok)
                            last = pe.matmul(psum[0:m, at:to], lhs[:, k, 0:m], ht[:, k, at:to],
                                             start=(k == 0), stop=(k == KD - 1))
                    last.then_inc(chunk_done, 1)

                for t in range(tiles):
                    pe.wait_ge(h_ready, t + 1)
                    if t >= 2:
                        pe.wait_ge(ht_ready, t - 1)
                    for k in range(KD):
                        last = pe.transpose(g.psum2(t % 2)[:, k * P:(k + 1) * P], h[:, t, k * P:(k + 1) * P], g.ident[:])
                    last.then_inc(transposed, 1)
                pe.wait_ge(ht_ready, tiles)
                with pe.Fori(0, looped // 2) as i:
                    for r in range(2):
                        pe.wait_ge(slab_loaded[r], i * 16 + 16)
                        pe.wait_ge(chunk_copied, i * 2 + (r + 1))
                        chunk(g.psum2(r), slab[:, r], P, wide)
                if which == 0:
                    pe.wait_ge(slab_loaded[0], 16 * (looped // 2 + 1))
                    pe.wait_ge(chunk_copied, looped + 1)
                    chunk(g.psum2(0), slab[:, 0], P, TOK)
                    pe.wait_ge(slab_loaded[1], 16 * (looped // 2 + 1))
                    pe.wait_ge(chunk_copied, looped + 2)
                    chunk(g.psum2(1), slab[:, 1], QK, TOK)
                    pe.wait_ge(rot_slab_ready, 2)
                    chunk(g.psum2(2), rot_slab, QK, SEQ)


@phase
def mix(g, l, proj, k_t, cat):
    nc, a = g.nc, g.a
    tag = f"{l}x"
    last_layer = l == DEPTH - 1
    tiles = NX if last_layer else NT
    W = tiles * P
    WA = W if last_layer else W + PAD_A
    WB = W if last_layer else W + PAD_B
    latent_squared, latent_summed, latent_mean, latent_root, latent_ready = g.sems(
        tag, "latent_squared", "latent_summed", "latent_mean", "latent_root", "latent_ready")
    v_done, v_copied, kv_loaded, padded, sigmoid_ready = g.sems(tag, "v_done", "v_copied", "kv_loaded", "padded", "sigmoid_ready")
    rot_built, qk_done, qk_copied, rope_done = g.sems(tag, "rot_built", "qk_done", "qk_copied", "rope_done")
    scored, shift_ready, exp_done, p_turned, pt_copied, pv_done, o_ready = g.sems(
        tag, "scored", "shift_ready", "exp_done", "p_turned", "pt_copied", "pv_done", "o_ready")
    conv_ready, conv_sum, conv_centred, conv_squared, conv_var, conv_root, conv_scaled = g.sems(
        tag, "conv_ready", "conv_sum", "conv_centred", "conv_squared", "conv_var", "conv_root", "conv_scaled")
    head_loaded = [g.sem(f"head_loaded_{tag}{e}") for e in range(2)]
    with ExitStack() as s:
        sb = lambda n, shape: s.enter_context(nc.sbuf_tensor(f"{n}_{tag}", shape, F32))
        wkv = sb("w_ukv", [P, HEADS, NOPE + VD])
        wq_head = sb("w_uq_head", [P, 2, 2, QK])
        wq_rot = sb("w_uq_rot", [P, 2, 2, QK])
        wk_head = sb("w_uk_head", [P, 2, NOPE])
        v = sb("v", [P, NT, HEADS * VD])
        q_t = sb("q_t", [P, 2, W])
        rot = sb("q_rot", [P, SEQ])
        prob = sb("prob", [P, 2, TOK])
        prob_t = sb("prob_t", [P, 2, TOK])
        o = sb("o", [P, tiles, 2 * VD])
        soft = sb("soft", [P, 4, 2 * NT])
        z_a = sb("z_a", [P, 2, TOK + 3 * PAD_A])
        z_b = sb("z_b", [P, 2, TOK + 3 * PAD_B])
        acc_b = sb("acc_b", [P, 2, TOK + PAD_B])
        work = sb("work", [P, 3, TOK + PAD_B])
        rstd = sb("rstd", [P, 2, TOK])
        newton = sb("newton", [P, TOK])
        taps = list(range(1, 3))
        PER_PAIR = (CONV_B - 3) // (HEADS // 2)
        per_pair_tiles = 2 * tiles
        turned_per_pair = per_pair_tiles + 1

        def streams(pad):
            yield slice(0, SEQ), slice(pad, pad + SEQ)
            if not last_layer:
                yield slice(SEQ, TOK), slice(2 * pad + SEQ, 2 * pad + TOK)

        def key_range(u):
            return (0, TOK) if u < NX else (SEQ, TOK)

        with nc.Block() as block:
            @block.sync
            def _(sp):
                sp.dma_start(wkv[:], a["w_ukv"][l].rearrange("p (h n) -> p h n", h=HEADS)).then_inc(kv_loaded, 16)
                wq = a["w_uq"][l].rearrange("(k p) n -> p k n", p=P)
                wk = a["w_ukv"][l]
                with sp.Fori(0, HEADS // 2) as i:
                    for e in range(2):
                        sp.wait_ge(qk_done, i * 2 + (e + 1))
                        sp.dma_start(wq_head[:, e], wq[:, :, bass.ds(i * (2 * QK) + e * QK, QK)]).then_inc(head_loaded[e], 16)
                        sp.dma_start(wk_head[:, e], wk[:, bass.ds(i * (2 * P) + e * P, NOPE)]).then_inc(head_loaded[e], 16)

            @block.gpsimd
            def _(pool):
                pool.memset(z_a[:], 0.0).then_inc(padded, 1)
                pool.memset(z_b[:], 0.0).then_inc(padded, 1)
                pool.memset(wq_rot[:], 0.0).then_inc(padded, 1)

            @block.scalar
            def _(act):
                act.sem_inc(pt_copied, 1)
                act.sem_inc(exp_done, 1)
                act.activation(work[:, 0:2, 0:W], proj[:, QCHUNK:QCHUNK + 2, 0:W], ACT.Square).then_inc(latent_squared, 1)
                act.activation(work[:, 2, 0:TOK], proj[:, KVCHUNK], ACT.Square).then_inc(latent_squared, 1)
                for n, (i, w_) in enumerate(((0, W), (1, TOK))):
                    act.wait_ge(latent_mean, n + 1)
                    act.activation(rstd[:, i, 0:w_], work[:, i, 0:w_], ACT.Sqrt).then_inc(latent_root, 1)
                act.activation(proj[:, 8:10, 0:W], proj[:, 8:10, 0:W], ACT.Sigmoid).then_inc(sigmoid_ready, 1)
                for t in range(NT):
                    act.wait_ge(v_done, t + 1)
                    act.activation(v[:, t], g.ps[:, 4 + t % 2], ACT.Copy).then_inc(v_copied, 1)
                with act.Fori(0, HEADS // 2) as i:
                    for e in range(2):
                        act.wait_ge(qk_done, i * 2 + (e + 3))
                        act.activation(q_t[0:NOPE, e], g.psum2(0)[0:NOPE, 0:W], ACT.Copy).then_inc(qk_copied, 1)
                        if not last_layer:
                            act.activation(q_t[NOPE:QK, e, SEQ:], g.psum2(0)[NOPE:QK, SEQ:TOK], ACT.Copy).then_inc(qk_copied, 1)
                        act.activation(k_t[0:NOPE, e], g.psum2(1)[0:NOPE, 0:TOK], ACT.Copy).then_inc(qk_copied, 1)
                        for u in range(tiles):
                            lo, hi = key_range(u)
                            n = e * tiles + u
                            act.wait_ge(shift_ready, i * per_pair_tiles + (n + 1))
                            act.activation(prob[:, n % 2, lo:hi], g.psum2(n % 2)[:, lo:hi], ACT.Exp, scale=SCALE,
                                           bias=soft[:, 1, n:n + 1], accum_out=soft[:, 2, n:n + 1]).then_inc(exp_done, 1)
                            act.wait_ge(p_turned, i * turned_per_pair + (n + 1))
                            act.activation(prob_t[:, n % 2, lo:hi], g.psum2(2)[:, lo:hi], ACT.Copy).then_inc(pt_copied, 1)
                    act.wait_ge(p_turned, i * turned_per_pair + turned_per_pair)
                    act.activation(cat[:, bass.ds(i + 4, 1), 0:W].rearrange("p c n -> p (c n)"), g.psum2(2)[:, 0:W],
                                   ACT.Copy).then_inc(pt_copied, 1)
                act.wait_ge(conv_centred, 1)
                act.activation(work[:, 0:2, 0:W], acc_b[:, :, 0:W], ACT.Square).then_inc(conv_squared, 1)
                act.wait_ge(conv_var, 1)
                act.activation(rstd[:, 0, 0:W], work[:, 2, 0:W], ACT.Sqrt).then_inc(conv_root, 1)
                for c in range(2):
                    act.wait_ge(conv_scaled, c + 1)
                    act.activation(cat[:, 2 + c, 0:W], cat[:, 2 + c, 0:W], ACT.Silu, scale=g.cols[:, c, 35:36],
                                   bias=g.cols[:, c, 36:37])

            @block.vector
            def _(dve):
                link = Links(dve, g.dve_step)
                dve.wait_ge(latent_summed, 1)
                dve.tensor_scalar(work[:, 0, 0:W], g.psum2(0)[:, 0:W], 1.0 / (2 * P), EPS, ALU.mult, ALU.add).then_inc(latent_mean, 1)
                dve.wait_ge(latent_summed, 2)
                dve.tensor_scalar(work[:, 1, 0:TOK], g.psum2(1)[:, 0:TOK], 1.0 / P, EPS, ALU.mult, ALU.add).then_inc(latent_mean, 1)

                def refined_rstd(i, at, w_):
                    y, t, v_ = rstd[:, i, 0:w_], newton[:, 0:w_], work[:, at, 0:w_]
                    link(dve.reciprocal(y, y))
                    link(dve.tensor_tensor(t, y, y, ALU.mult))
                    link(dve.tensor_tensor(t, t, v_, ALU.mult))
                    link(dve.tensor_scalar(t, t, -0.5, 1.5, ALU.mult, ALU.add))
                    link(dve.tensor_tensor(y, y, t, ALU.mult))

                dve.wait_ge(latent_root, 1)
                refined_rstd(0, 0, W)
                for c in range(2):
                    dve.scalar_tensor_tensor(proj[:, QCHUNK + c, 0:W], proj[:, QCHUNK + c, 0:W], g.cols[:, c, 37:38],
                                             rstd[:, 0, 0:W], ALU.mult, ALU.mult).then_inc(latent_ready, 1)
                dve.wait_ge(latent_root, 2)
                refined_rstd(1, 1, TOK)
                dve.scalar_tensor_tensor(proj[:, KVCHUNK], proj[:, KVCHUNK], g.kvg[:, 0:1], rstd[:, 1], ALU.mult,
                                         ALU.mult).then_inc(latent_ready, 1)
                dve.wait_ge(padded, 3)
                dve.wait_ge(sigmoid_ready, 1)
                for tok, at in streams(PAD_A):
                    link.mark(dve.tensor_tensor(z_a[:, :, at], proj[:, 2:4, tok], proj[:, 4:6, tok], ALU.mult))
                for tok, at in streams(PAD_B):
                    link.mark(dve.tensor_tensor(z_b[:, :, at], proj[:, 6:8, tok], proj[:, 8:10, tok], ALU.mult))
                link.wait()
                acc_a = work[:, 1:3, 0:WA]
                for c in range(2):
                    link.mark(dve.tensor_scalar(acc_a[:, c], z_a[:, c, 0:WA], g.cols[:, c, 0:1], None, ALU.mult))
                for k in range(1, CONV_A):
                    for c in range(2):
                        link.wait(1)
                        link.mark(dve.scalar_tensor_tensor(acc_a[:, c], z_a[:, c, k:k + WA], g.cols[:, c, k:k + 1],
                                                           acc_a[:, c], ALU.mult, ALU.add))
                link.wait()
                for tok, at in streams(PAD_A):
                    out_at = slice(at.start - PAD_A, at.stop - PAD_A)
                    link.mark(dve.tensor_tensor(cat[:, 0:2, tok], proj[:, 0:2, tok], acc_a[:, :, out_at], ALU.mult))

                def tap(k, c):
                    link.wait(1)
                    at = bass.ds(k, WB)
                    w_at = bass.ds(k + CONV_A, 1)
                    link.mark(dve.scalar_tensor_tensor(acc_b[:, c, 0:WB], z_b[:, c, at], g.cols[:, c, w_at],
                                                       acc_b[:, c, 0:WB], ALU.mult, ALU.add))

                for c in range(2):
                    link.mark(dve.tensor_scalar(acc_b[:, c, 0:WB], z_b[:, c, 0:WB], g.cols[:, c, CONV_A:CONV_A + 1],
                                                g.cols[:, c, 34:35], ALU.mult, ALU.add))
                for k in taps:
                    for c in range(2):
                        tap(k, c)
                link.reset()
                rp = slice(NOPE, QK)
                with dve.Fori(0, HEADS // 2) as i:
                    todo = [(k, c) for k in range(PER_PAIR) for c in range(2)]
                    total = len(todo)

                    def o_part(n):
                        e, u = divmod(n, tiles)
                        dve.wait_ge(pv_done, i * per_pair_tiles + (n + 1))
                        link(dve.reciprocal(soft[:, 3, n:n + 1], soft[:, 2, n:n + 1]))
                        dve.tensor_scalar(o[:, u, e * VD:(e + 1) * VD], g.ps[:, 6 + n % 2, 0:VD],
                                          soft[:, 3, n:n + 1], None, ALU.mult).then_inc(o_ready, 1)

                    for e in range(2):
                        dve.wait_ge(head_loaded[e], i * 32 + 32)
                        src = wq_head[:, e, :, NOPE:QK].rearrange("p k (s u e) -> p k s u e", s=2, u=2)
                        dst = wq_rot[:, e, :, NOPE:QK].rearrange("p k (s u e) -> p k s u e", s=2, u=2)
                        dve.tensor_scalar(dst[:, :, :, 0], src[:, :, :, 1], -1.0, None, ALU.mult).then_inc(rot_built, 1)
                        dve.tensor_copy(dst[:, :, :, 1], src[:, :, :, 0]).then_inc(rot_built, 1)
                        dve.wait_ge(qk_done, i * 2 + (e + 3))
                        link.mark(dve.tensor_tensor(rot[rp], g.psum2(2)[rp, 0:SEQ], g.rope[rp, 1], ALU.mult))
                        link(dve.tensor_tensor(q_t[rp, e, 0:SEQ], g.psum2(0)[rp, 0:SEQ], g.rope[rp, 0], ALU.mult))
                        dve.tensor_tensor(q_t[rp, e, 0:SEQ], q_t[rp, e, 0:SEQ], rot[rp], ALU.add).then_inc(rope_done, 1)
                        for u in range(tiles):
                            lo, hi = key_range(u)
                            n = e * tiles + u
                            dve.wait_ge(scored, i * per_pair_tiles + (n + 1))
                            link(dve.tensor_reduce(soft[:, 0, n:n + 1], g.psum2(n % 2)[:, lo:hi], AX_X, ALU.max))
                            dve.tensor_scalar(soft[:, 1, n:n + 1], soft[:, 0, n:n + 1], -SCALE, None, ALU.mult
                                              ).then_inc(shift_ready, 1)
                            while total - len(todo) < (n + 1) * total // per_pair_tiles:
                                k, c = todo.pop(0)
                                tap(i * PER_PAIR + (3 + k), c)
                            if u >= 2:
                                o_part(n - 2)
                        o_part(n - 1)
                        o_part(n)
                    link.reset()
                dve.tensor_copy(acc_b[:, 0, 0:1], acc_b[:, 0, 0:1]).then_inc(conv_ready, 1)
                dve.wait_ge(conv_sum, 1)
                link(dve.tensor_scalar(work[:, 2, 0:W], g.psum2(0)[:, 0:W], 1.0 / (2 * P), None, ALU.mult))
                for c in range(2):
                    for tok, at in streams(PAD_B):
                        out_at = slice(at.start - PAD_B, at.stop - PAD_B)
                        link(dve.tensor_tensor(cat[:, 2 + c, tok], acc_b[:, c, out_at], work[:, 2, tok], ALU.subtract))
                dve.tensor_copy(acc_b[:, :, 0:W], cat[:, 2:4, 0:W]).then_inc(conv_centred, 1)
                dve.wait_ge(conv_sum, 2)
                dve.tensor_scalar(work[:, 2, 0:W], g.psum2(1)[:, 0:W], 1.0 / (2 * P), EPS, ALU.mult, ALU.add).then_inc(conv_var, 1)
                dve.wait_ge(conv_root, 1)
                refined_rstd(0, 2, W)
                for c in range(2):
                    dve.tensor_tensor(cat[:, 2 + c, 0:W], cat[:, 2 + c, 0:W], rstd[:, 0, 0:W], ALU.mult).then_inc(conv_scaled, 1)
                link.reset()

            @block.tensor
            def _(pe):
                def spans(n_tok):
                    return [(at, min(at + 512, n_tok)) for at in range(0, n_tok, 512)]

                pe.sem_inc(qk_done, 2)
                pe.wait_ge(latent_squared, 1)
                for c in range(2):
                    for lo, hi in spans(W):
                        last = pe.matmul(g.psum2(0)[:, lo:hi], g.ones[:], work[:, c, lo:hi], start=(c == 0), stop=(c == 1))
                last.then_inc(latent_summed, 1)
                pe.wait_ge(latent_squared, 2)
                for lo, hi in spans(TOK):
                    last = pe.matmul(g.psum2(1)[:, lo:hi], g.ones[:], work[:, 2, lo:hi], start=True, stop=True)
                last.then_inc(latent_summed, 1)
                pe.wait_ge(latent_ready, 3)
                pe.wait_ge(kv_loaded, 16)
                for t in range(NT):
                    if t >= 2:
                        pe.wait_ge(v_copied, t - 1)
                    pe.matmul(g.ps[:, 4 + t % 2], proj[:, KVCHUNK, t * P:(t + 1) * P], wkv[:, :, NOPE:],
                              start=True, stop=True).then_inc(v_done, 1)
                pe.wait_ge(v_copied, NT)
                with pe.Fori(0, HEADS // 2) as i:
                    copies = 2 if last_layer else 3
                    for e in range(2):
                        n0 = e * tiles
                        pe.wait_ge(head_loaded[e], i * 32 + 32)
                        pe.wait_ge(rot_built, i * 4 + (2 * e + 2))
                        pe.wait_ge(exp_done, i * per_pair_tiles + (n0 + 1))
                        pe.wait_ge(pt_copied, i * turned_per_pair + (n0 + 1))
                        for k in range(2):
                            for lo, hi in spans(W):
                                pe.matmul(g.psum2(0)[0:QK, lo:hi], wq_head[:, e, k, :], proj[:, QCHUNK + k, lo:hi],
                                          start=(k == 0), stop=(k == 1))
                            pe.matmul(g.psum2(2)[0:QK, 0:SEQ], wq_rot[:, e, k, :], proj[:, QCHUNK + k, 0:SEQ],
                                      start=(k == 0), stop=(k == 1))
                        for lo, hi in spans(TOK):
                            last = pe.matmul(g.psum2(1)[0:NOPE, lo:hi], wk_head[:, e, :], proj[:, KVCHUNK, lo:hi],
                                             start=True, stop=True)
                        last.then_inc(qk_done, 1)
                        pe.wait_ge(qk_copied, i * (2 * copies) + copies * (e + 1))
                        pe.wait_ge(rope_done, i * 2 + (e + 1))

                        def score(u):
                            n = n0 + u
                            if u >= 2:
                                pe.wait_ge(exp_done, i * per_pair_tiles + n)
                            lo, hi = key_range(u)
                            for at in range(lo, hi, 512):
                                to = min(at + 512, hi)
                                last = pe.matmul(g.psum2(n % 2)[:, at:to], q_t[0:QK, e, u * P:(u + 1) * P],
                                                 k_t[0:QK, e, at:to], start=True, stop=True)
                            last.then_inc(scored, 1)

                        def turn(u):
                            n = n0 + u
                            lo, hi = key_range(u)
                            pe.wait_ge(exp_done, i * per_pair_tiles + (n + 2))
                            pe.wait_ge(pt_copied, i * turned_per_pair + (n + 1))
                            for at in range(lo, hi, P):
                                last = pe.transpose(g.psum2(2)[:, at:at + P], prob[:, n % 2, at:at + P], g.ident[:])
                            last.then_inc(p_turned, 1)

                        def weigh(u):
                            n = n0 + u
                            lo, hi = key_range(u)
                            pe.wait_ge(pt_copied, i * turned_per_pair + (n + 2))
                            if n >= 2:
                                pe.wait_ge(o_ready, i * per_pair_tiles + (n - 1))
                            for at in range(lo, hi, P):
                                last = pe.matmul(g.ps[:, 6 + n % 2, 0:VD], prob_t[:, n % 2, at:at + P],
                                                 v[:, at // P, bass.ds(i * (2 * VD) + e * VD, VD)],
                                                 start=(at == lo), stop=(at + P == hi))
                            last.then_inc(pv_done, 1)

                        score(0)
                        for u in range(tiles):
                            if u + 1 < tiles:
                                score(u + 1)
                            if u >= 1:
                                weigh(u - 1)
                            turn(u)
                        weigh(tiles - 1)
                    pe.wait_ge(o_ready, i * per_pair_tiles + per_pair_tiles)
                    for u in range(tiles):
                        last = pe.transpose(g.psum2(2)[:, u * P:(u + 1) * P], o[:, u, :], g.ident[:])
                    last.then_inc(p_turned, 1)
                pe.wait_ge(conv_ready, 1)
                for c in range(2):
                    for tok, at in streams(PAD_B):
                        out_at = slice(at.start - PAD_B, at.stop - PAD_B)
                        last = pe.matmul(g.psum2(0)[:, tok], g.ones[:], acc_b[:, c, out_at], start=(c == 0), stop=(c == 1))
                last.then_inc(conv_sum, 1)
                pe.wait_ge(conv_squared, 1)
                for c in range(2):
                    for lo, hi in spans(W):
                        last = pe.matmul(g.psum2(1)[:, lo:hi], g.ones[:], work[:, c, lo:hi], start=(c == 0), stop=(c == 1))
                last.then_inc(conv_sum, 1)


@phase
def project_out(g, l, cat):
    nc, a = g.nc, g.a
    tiles = NX if l == DEPTH - 1 else NT
    w_loaded, tile_done, tile_scaled, = g.sems(f"{l}o", "w_loaded", "tile_done", "tile_scaled")
    with ExitStack() as s:
        w = s.enter_context(nc.sbuf_tensor(f"w_out_{l}", [P, KD, D], F32))
        with nc.Block() as block:
            @block.sync
            def _(sp):
                sp.dma_start(w[:], a["w_out"][l].rearrange("(k p) n -> p k n", p=P)).then_inc(w_loaded, 16)

            @block.tensor
            def _(pe):
                pe.wait_ge(w_loaded, 16)
                for t in range(tiles):
                    if t >= 2:
                        pe.wait_ge(tile_scaled, t - 1)
                    for k in range(KD):
                        for b in range(2):
                            last = pe.matmul(g.psum2(t % 2)[:, b * 512:(b + 1) * 512], cat[:, k, t * P:(t + 1) * P],
                                             w[:, k, b * 512:(b + 1) * 512], start=(k == 0), stop=(k == KD - 1))
                    last.then_inc(tile_done, 1)

            @block.vector
            def _(dve):
                link = Links(dve, g.dve_step)
                for t in range(tiles):
                    st = 0 if t < NX else 1
                    dve.wait_ge(tile_done, t + 1)
                    dve.tensor_tensor(g.rows[:, 0, 0], g.psum2(t % 2), g.rows[:, st, 2], ALU.mult).then_inc(tile_scaled, 1)
                    dve.wait_ge(tile_scaled, t + 1)
                    link(dve.tensor_tensor(g.x[:, t], g.x[:, t], g.rows[:, 0, 0], ALU.add))
                link.reset()


@phase
def peer(g, l, tiles, h, ht, q_t, keys_t):
    nc, a = g.nc, g.a
    tag = f"{l}p"
    groups = tiles * PH
    (scored, ranked, idx_ready, best_ready, gate_ready, dotted, acted, weighted, diag_ready, v_used) = g.sems(tag, "scored", "ranked", "idx_ready", "best_ready", "gate_ready", "dotted",
                       "acted", "weighted", "diag_ready", "v_used")
    q_done, q_copied, summed = g.sems(tag, "q_done", "q_copied", "summed")
    slab_loaded = [g.sem(f"slab_loaded_{tag}{r}") for r in range(2)]
    u_loaded = [g.sem(f"u_loaded_{tag}{n}") for n in range(NU)]
    v_loaded = [g.sem(f"v_loaded_{tag}{n}") for n in range(NV)]
    NDIAG = 4
    with ExitStack() as s:
        sb = lambda n, shape, dt=F32: s.enter_context(nc.sbuf_tensor(f"{n}_{tag}", shape, dt))
        u_buf = sb("u_rows", [P, NU, D])
        v_buf = sb("v_rows", [P, NV - 2, D])
        slab = sb("q_slab", [P, 2, KD, P])
        v_at = [v_buf[:, n] for n in range(NV - 2)] + [g.rows[:, 1, 0], g.rows[:, 1, 1]]
        scaled = g.rows[:, 0, 1]
        left = sb("left", [P, 2, P])
        top = sb("top", [P, 2, TOPK])
        top_i = sb("top_i", [P, 2, TOPK], U32)
        top_f = sb("top_f", [P, 2, TOPK])
        cand = sb("cand", [P, 2, TOPK * TOPK])
        best = sb("best", [P, 2, TOPK])
        best_i = sb("best_i", [P, TOPK], U32)
        pair_i = sb("pair_i", [P, 2, TOPK], U32)
        pair_f = sb("pair_f", [P, 2, TOPK])
        match = sb("match", [P, 2, TOPK, TOPK])
        found = sb("found", [P, 2, TOPK])
        shift = sb("shift", [P, 2, 1])
        total = sb("total", [P, 2, 2])
        idx = sb("idx", [P, tiles, TOPK], U32)
        gate = sb("gate", [P, 2, TOPK])
        dots = sb("dots", [P, 2, TOPK])
        gelu = sb("gelu", [P, 2, TOPK])
        wts = sb("wts", [P, 2, TOPK])
        diag = sb("diag", [P, NDIAG, P])

        def exists(b, k):
            return not isinstance(b, int) or b * tiles + k < groups

        def each_head(eng, body):
            with eng.Fori(0, PH - 1) as b:
                body(b)
            body(PH - 1)

        with nc.Block() as block:
            @block.sync
            def _(sp):
                with sp.Fori(0, PH - 1) as b:
                    for r in range(2):
                        sp.wait_ge(q_done, b * 2 + (r + 1))
                        sp.dma_start(slab[:, r], a["peer_w_q"][l, bass.ds(b * 2 + (r + 2), 1)].rearrange(
                            "c p k n -> p (c k) n")).then_inc(slab_loaded[r], 16)

            @block.gpsimd
            def _(pool):
                def gather(buf, table, k, j, loaded):
                    pool.nop(nofuse=True)
                    pool.indirect_dma_start(buf, None, table.rearrange("l e d -> (l e) d"),
                                            bass.IndirectOffsetOnAxis(idx[:, k % tiles, j:j + 1], 0),
                                            element_offset=l * NKEY * NKEY * D).then_inc(loaded, 16)

                pool.wait_ge(idx_ready, 1)
                for j in range(TOPK):
                    if j >= NU:
                        pool.wait_ge(dotted, j - NU + 1)
                    gather(u_buf[:, j % NU], a["peer_u"], 0, j, u_loaded[j % NU])

                def body(b):
                    for k in range(tiles):
                        with_u = exists(b, k + 1)
                        if with_u:
                            pool.wait_ge(idx_ready, b * tiles + (k + 2))
                        for j in range(TOPK):
                            if with_u:
                                pool.wait_ge(dotted, b * (tiles * TOPK) + ((k + 1) * TOPK + j - NU + 1))
                                gather(u_buf[:, j % NU], a["peer_u"], k + 1, j, u_loaded[j % NU])
                            pool.wait_ge(v_used, b * (tiles * TOPK) + (k * TOPK + j + 1))
                            gather(v_at[j % NV], a["peer_v"], k, j, v_loaded[j % NV])

                each_head(pool, body)

            @block.scalar
            def _(act):
                def gates(b, k):
                    if not exists(b, k):
                        return
                    act.wait_ge(best_ready, b * tiles + (k + 1))
                    act.activation(gate[:, k % 2], best[:, k % 2], ACT.Exp, bias=shift[:, k % 2],
                                   accum_out=total[:, k % 2, 0:1]).then_inc(gate_ready, 1)

                gates(0, 0)

                def body(b):
                    for k in range(tiles):
                        if k == tiles - 2 and exists(b, tiles):
                            act.wait_ge(scored, b * tiles + tiles)
                            for c in range(2):
                                act.wait_ge(q_done, b * 2 + (c + 3))
                                act.activation(q_t[:, c], g.psum2(2 + c)[:, 0:tiles * P], ACT.Copy).then_inc(q_copied, 1)
                        gates(b, k + 1)
                        act.wait_ge(dotted, b * (tiles * TOPK) + (k + 1) * TOPK)
                        act.activation(gelu[:, k % 2], dots[:, k % 2], ACT.Gelu).then_inc(acted, 1)
                        act.wait_ge(weighted, b * tiles + (k + 1))
                        for j in range(TOPK):
                            act.wait_ge(v_used, b * (tiles * TOPK) + (k * TOPK + j + 1 - NDIAG + NV))
                            act.activation(diag[:, j % NDIAG], g.ident[:], ACT.Copy, scale=wts[:, k % 2, j:j + 1]
                                           ).then_inc(diag_ready, 1)

                each_head(act, body)

            @block.vector
            def _(dve):
                link = Links(dve, g.dve_step)

                def route(b, k):
                    if not exists(b, k):
                        return
                    r = k % 2
                    dve.wait_ge(scored, b * tiles + (k + 1))
                    dve.nop(nofuse=True)
                    for p in range(2):
                        sc = g.ps[:, r, p * P:(p + 1) * P]
                        link(dve.max(top[:, p, 0:8], sc))
                        link.mark(dve.max_index(top_i[:, p, 0:8], top[:, p, 0:8], sc))
                        link(dve.match_replace(left[:, p], top[:, p, 0:8], sc, LOWEST))
                        link(dve.max(top[:, p, 8:16], left[:, p]))
                        dve.max_index(top_i[:, p, 8:16], top[:, p, 8:16], left[:, p]).then_inc(ranked, 1)
                    dve.wait_ge(ranked, b * (2 * tiles) + (2 * k + 2))
                    link.mark(dve.tensor_tensor(cand[:, 0].rearrange("p (i j) -> p i j", i=TOPK),
                                                top[:, 0].unsqueeze(2).broadcast_to([P, TOPK, TOPK]),
                                                top[:, 1].unsqueeze(1).broadcast_to([P, TOPK, TOPK]), ALU.add))
                    link(dve.tensor_copy(top_f[:], top_i[:]))
                    link(dve.max(best[:, r, 0:8], cand[:, 0]))
                    link.mark(dve.max_index(best_i[:, 0:8], best[:, r, 0:8], cand[:, 0]))
                    link(dve.match_replace(cand[:, 1], best[:, r, 0:8], cand[:, 0], LOWEST))
                    link(dve.max(best[:, r, 8:16], cand[:, 1]))
                    link.mark(dve.max_index(best_i[:, 8:16], best[:, r, 8:16], cand[:, 1]))
                    dve.tensor_scalar(shift[:, r], best[:, r, 0:1], -1.0, None, ALU.mult).then_inc(best_ready, 1)
                    link.wait()
                    link.mark(dve.tensor_scalar(pair_i[:, 0], best_i[:], 4, None, ALU.logical_shift_right))
                    link(dve.tensor_scalar(pair_i[:, 1], best_i[:], TOPK - 1, None, ALU.bitwise_and))
                    link(dve.tensor_copy(pair_f[:], pair_i[:]))
                    for p in range(2):
                        link.mark(dve.tensor_tensor(match[:, p], pair_f[:, p].unsqueeze(2).broadcast_to([P, TOPK, TOPK]),
                                                    g.iota[:].unsqueeze(1).broadcast_to([P, TOPK, TOPK]), ALU.is_equal))
                    for p in range(2):
                        link.wait(1)
                        link.mark(dve.tensor_tensor(match[:, p], match[:, p],
                                                    top_f[:, p].unsqueeze(1).broadcast_to([P, TOPK, TOPK]), ALU.mult))
                    link.wait()
                    link(dve.tensor_reduce(found[:], match[:], AX_X, ALU.add))
                    dve.scalar_tensor_tensor(idx[:, k % tiles], found[:, 0], float(NKEY), found[:, 1], ALU.mult, ALU.add
                                             ).then_inc(idx_ready, 1)

                route(0, 0)
                link.reset()

                def body(b):
                    for k in range(tiles):
                        r = k % 2
                        route(b, k + 1)
                        for j in range(TOPK):
                            dve.wait_ge(u_loaded[j % NU], b * (16 * tiles * TOPK // NU) + 16 * ((k * TOPK + j) // NU + 1))
                            dve.tensor_tensor_reduce(u_buf[:, j % NU], u_buf[:, j % NU], h[:, k], 1.0, 0.0, ALU.mult,
                                                     ALU.add, dots[:, r, j:j + 1]).then_inc(dotted, 1)
                        dve.wait_ge(gate_ready, b * tiles + (k + 1))
                        link(dve.reciprocal(total[:, r, 1:2], total[:, r, 0:1]))
                        dve.wait_ge(acted, b * tiles + (k + 1))
                        dve.scalar_tensor_tensor(wts[:, r], gelu[:, r], total[:, r, 1:2], gate[:, r], ALU.mult, ALU.mult
                                                 ).then_inc(weighted, 1)
                        update(b, k)
                    link.reset()

                def update(b, k):
                    t = (k - 1) % tiles
                    dve.wait_ge(v_used, b * (tiles * TOPK) + (k * TOPK + NV))
                    dve.tensor_tensor(scaled, g.psum2(1), g.rows[:, 0 if t < NX else 1, 2], ALU.mult).then_inc(summed, 1)
                    dve.wait_ge(summed, b * tiles + (k + 1))
                    link(dve.tensor_tensor(g.x[:, t], g.x[:, t], scaled, ALU.add))

                link(dve.memset(g.psum2(1), 0.0))
                link.reset()
                each_head(dve, body)
                update(PH - 1, tiles)
                link.reset()

            @block.tensor
            def _(pe):
                pe.sem_inc(v_used, NV)
                pe.sem_inc(q_done, 2)
                pe.sem_inc(q_copied, 2)
                every = (tiles - 2) * TOPK // (2 * KD)

                def scores(b, k):
                    if not exists(b, k):
                        return
                    head, t = b + k // tiles, k % tiles
                    if k == tiles:
                        pe.wait_ge(q_copied, b * 2 + 4)
                    if not (isinstance(b, int) and b * tiles + k < 2):
                        pe.wait_ge(ranked, b * (2 * tiles) + 2 * (k - 1))
                    for p in range(2):
                        last = pe.matmul(g.ps[:, k % 2, p * P:(p + 1) * P], q_t[:, p, t * P:(t + 1) * P],
                                         keys_t[:, bass.ds(head * 2 + p, 1)].rearrange("p c n -> p (c n)"),
                                         start=True, stop=True)
                    last.then_inc(scored, 1)

                def project(b, n):
                    c, k = divmod(n, KD)
                    if k == 0:
                        pe.wait_ge(slab_loaded[c], b * 16 + 16)
                        pe.wait_ge(q_copied, b * 2 + 2)
                    for lo in range(0, tiles * P, 512):
                        hi = min(lo + 512, tiles * P)
                        last = pe.matmul(g.psum2(2 + c)[:, lo:hi], slab[:, c, k], ht[:, k, lo:hi],
                                         start=(k == 0), stop=(k == KD - 1))
                    if k == KD - 1:
                        last.then_inc(q_done, 1)

                scores(0, 0)
                scores(0, 1)

                def body(b):
                    for k in range(tiles):
                        scores(b, k + 2)
                        pe.wait_ge(summed, b * tiles + (k + 1))
                        for j in range(TOPK):
                            f = k * TOPK + j
                            pe.wait_ge(v_loaded[j % NV], b * (16 * tiles * TOPK // NV) + 16 * (f // NV + 1))
                            pe.wait_ge(diag_ready, b * (tiles * TOPK) + (f + 1))
                            for c in range(2):
                                last = pe.matmul(g.psum2(1)[:, c * 512:(c + 1) * 512], diag[:, j % NDIAG],
                                                 v_at[j % NV][:, c * 512:(c + 1) * 512], start=(j == 0),
                                                 stop=(j == TOPK - 1))
                            last.then_inc(v_used, 1)
                            if exists(b, tiles) and f % every == every - 1 and f // every < 2 * KD:
                                project(b, f // every)

                each_head(pe, body)


@phase
def final_norm(g):
    nc, a = g.nc, g.a
    row_loaded, squared, mean_ready, rstd_ready, tile_ready, stored = g.sems(
        "f", "row_loaded", "squared", "mean_ready", "rstd_ready", "tile_ready", "stored")
    with ExitStack() as s:
        sb = lambda n, shape: s.enter_context(nc.sbuf_tensor(n, shape, F32))
        grow, y, stat = sb("final_row", [P, D]), sb("final", [P, NX, D]), sb("final_stat", [P, 3, NX])
        with nc.Block() as block:
            @block.sync
            def _(sp):
                sp.dma_start(grow[:], a["final_norm_g"].partition_broadcast(P)).then_inc(row_loaded, 16)
                for t in range(NX):
                    sp.wait_ge(tile_ready, t + 1)
                    sp.dma_start(a["out"][0, t * P:(t + 1) * P, :], y[:, t]).then_inc(stored, 16)
                sp.wait_ge(stored, 16 * NX)

            @block.scalar
            def _(act):
                for t in range(NX):
                    act.activation(y[:, t], g.x[:, t], ACT.Square, accum_out=stat[:, 0, t:t + 1]).then_inc(squared, 1)

            @block.gpsimd
            def _(pool):
                pool.wait_ge(mean_ready, 1)
                pool.tensor_tensor(stat[:, 2], stat[:, 1], g.half[:, 0:NX], ALU.pow).then_inc(rstd_ready, 1)

            @block.vector
            def _(dve):
                dve.wait_ge(squared, NX)
                dve.tensor_scalar(stat[:, 1], stat[:, 0], 1.0 / D, EPS, ALU.mult, ALU.add).then_inc(mean_ready, 1)
                dve.wait_ge(rstd_ready, 1)
                dve.wait_ge(row_loaded, 16)
                for t in range(NX):
                    dve.scalar_tensor_tensor(y[:, t], g.x[:, t], stat[:, 2, t:t + 1], grow[:], ALU.mult, ALU.mult
                                             ).then_inc(tile_ready, 1)


def trunk(nc, a):
    with ExitStack() as stack:
        g = Program(nc, stack, a)
        modulation(g)
        for l in range(DEPTH):
            last_layer = l == DEPTH - 1
            with ExitStack() as s:
                sb = lambda n, shape: s.enter_context(nc.sbuf_tensor(f"{n}_{l}", shape, F32))
                k_t = sb("k_t", [P, 2, TOK])
                cat = sb("cat", [P, KD, NX * P if last_layer else TOK])
                with ExitStack() as s2:
                    proj = s2.enter_context(nc.sbuf_tensor(f"proj_{l}", [P, NPROJ, TOK], F32))
                    with (nc.sbuf_tensor(f"h1_{l}", [P, NT, D], F32) as h,
                          nc.sbuf_tensor(f"h1_t_{l}", [P, KD, TOK], F32) as ht):
                        norm_and_project(g, l, 0, NT, h, {"h_t": ht, "proj": proj, "k_t": k_t})
                    mix(g, l, proj, k_t, cat)
                project_out(g, l, cat)
            tiles = NX if last_layer else NT
            with ExitStack() as s:
                sb = lambda n, shape: s.enter_context(nc.sbuf_tensor(f"{n}_{l}", shape, F32))
                h = sb("h2", [P, tiles, D])
                ht = sb("h_t", [P, KD, tiles * P])
                q_t = sb("peer_q_t", [P, 2, tiles * P])
                keys_t = sb("keys_t", [P, 2 * PH, P])
                norm_and_project(g, l, 1, tiles, h, {"h_t": ht, "proj": q_t, "keys_t": keys_t})
                peer(g, l, tiles, h, ht, q_t, keys_t)
        final_norm(g)


_INS = ["x", "c", "ctx", "c_ctx", "w_mod", "b_mod", "norm1_g", "norm2_g", "w_in", "w_out", "conv_a_w", "conv_b_w",
        "conv_b_bias", "conv_b_ln_g", "conv_b_ln_b", "mla_q_norm_g", "w_uq", "mla_kv_norm_g", "w_ukv", "peer_w_q",
        "peer_sub_keys", "peer_u", "peer_v", "final_norm_g"]


def shape_constants():
    axis = ROPE // 2
    inv = (ROPE_BASE ** (-np.arange(0, axis, 2, dtype=np.float32) / axis)).astype(np.float32)
    n = np.arange(SEQ)
    ar = (n // GRID_W).astype(np.float32)[:, None] * inv
    ac = (n % GRID_W).astype(np.float32)[:, None] * inv
    ang = np.concatenate([ar, ar, ac, ac], axis=-1).T
    tables = np.stack([np.cos(ang), np.sin(ang)], axis=1).astype(np.float32)
    return {"identity": np.eye(P, dtype=np.float32), "rope_tables": np.ascontiguousarray(tables)}


def kernel(**inputs):
    import concourse.bacc as _bacc
    from concourse.bass_utils import run_bass_kernel_spmd as _run

    nc = _bacc.Bacc("TRN2", target_bir_lowering=False, num_devices=1)
    arrays, args = {}, {}
    host = {n: np.ascontiguousarray(inputs[n]) for n in _INS}
    host["peer_w_q"] = np.ascontiguousarray(
        host["peer_w_q"].reshape(DEPTH, KD, P, 2 * PH, P).transpose(0, 3, 2, 1, 4))
    host["peer_sub_keys"] = np.ascontiguousarray(
        host["peer_sub_keys"].reshape(DEPTH, 2 * PH, NKEY, P).transpose(0, 3, 1, 2))
    host.update(shape_constants())
    for name, v in host.items():
        arrays[f"in_{name}"] = v
        args[name] = nc.dram_tensor(f"in_{name}", v.shape, mybir.dt.from_np(v.dtype), kind="ExternalInput").ap()
    args["out"] = nc.dram_tensor("out_0", (1, SEQ, D), F32, kind="ExternalOutput").ap()
    trunk(nc, args)
    r = _run(nc, [arrays], core_ids=[0])
    return r.results[0]["out_0"]
```

```python
from contextlib import ExitStack

import numpy as np

import concourse.bass as bass
from concourse import mybir

F32 = mybir.dt.float32
U32 = mybir.dt.uint32
ALU = mybir.AluOpType
ACT = mybir.ActivationFunctionType
AX_X = mybir.AxisListType.X

P = 128
D = 1024
KD = D // P
DEPTH = 2
SEQ, CTX = 512, 256
TOK = SEQ + CTX
NX, NT = SEQ // P, TOK // P
HEADS, NOPE, ROPE, VD = 8, 64, 32, 64
QK = NOPE + ROPE
SCALE = QK ** -0.5
CONV_A, CONV_B = 3, 31
PAD_A, PAD_B = CONV_A // 2, CONV_B // 2
QCHUNK, KVCHUNK, KRCHUNK = 10, 12, 13
NPROJ = 13
EPS = 1e-6
PH, NKEY, TOPK = 8, 128, 16
LOWEST = -3.0e38
NU = NV = 8
SLABS = 3
GRID_W, ROPE_BASE = 64, 10000.0
FIRST = 2


class Links:

    def __init__(self, eng, sem):
        self.eng, self.sem, self.n = eng, sem, 0

    def mark(self, ins):
        self.n += 1
        ins.then_inc(self.sem, 1)

    def wait(self, behind=0):
        if self.n > behind:
            self.eng.wait_ge(self.sem, self.n - behind)

    def __call__(self, ins):
        self.mark(ins)
        self.wait()

    def reset(self):
        self.wait()
        if self.n:
            self.eng.sem_clear(self.sem)
        self.n = 0


class Program:

    def __init__(self, nc, stack, a):
        self.nc, self.stack, self.a = nc, stack, a
        sb = self.sb
        self.x = sb("x_tiles", [P, NT, D])
        self.rows = sb("mod_rows", [P, 2, 3, D])
        self.ident = sb("ident", [P, P])
        self.ones = sb("ones", [P, P])
        self.rope = sb("rope", [P, SEQ])
        self.half = sb("minus_half", [P, NT])
        self.iota = sb("iota16", [P, TOPK])
        self.cols = sb("cols", [P, 2, 38])
        self.kvg = sb("kv_norm_g", [P, 1])
        self.ps = stack.enter_context(nc.psum_tensor("psum", [P, 8, 512], F32))
        self.mod_dram = nc.dram_tensor("mod_dram", (2, DEPTH * 6 * D), F32, kind="Internal").ap()
        self.dve_step = stack.enter_context(nc.semaphore("dve_step"))

    def sb(self, name, shape, dt=F32):
        return self.stack.enter_context(self.nc.sbuf_tensor(name, shape, dt))

    def sem(self, name):
        self.phase_sems.append(self.sem_stack.enter_context(self.nc.semaphore(name)))
        return self.phase_sems[-1]

    def sems(self, tag, *names):
        return [self.sem(f"{n}_{tag}") for n in names]

    def psum2(self, b):
        return self.ps[:, 2 * b:2 * b + 2, :].rearrange("p b n -> p (b n)")


def phase(build):
    def run(g, *args):
        with ExitStack() as g.sem_stack:
            g.phase_sems = []
            build(g, *args)
            numbers = sorted(x.num for x in g.phase_sems)
            starts = [n for n in numbers if n - 1 not in numbers]
            ends = [n + 1 for n in numbers if n + 1 not in numbers]
            for first, end in zip(starts, ends):
                g.nc.gpsimd.sem_clear(range(first, end))
            g.nc.all_engine_barrier()
    return run


def load_mod_rows(g, sp, l, which, rows, loaded):
    at = (l * 6 + which * 3) * D
    for s in range(2):
        sp.dma_start(g.rows[:, s, rows.start:rows.stop].rearrange("p r n -> p (r n)"),
                     g.mod_dram[s, at + rows.start * D:at + rows.stop * D].partition_broadcast(P)).then_inc(loaded, 16)


@phase
def modulation(g):
    nc, a = g.nc, g.a
    NCH = 6 * D // 512
    tensors_loaded, c_ready, row_done, row_added, rows_out = g.sems("m", "tensors_loaded", "c_ready", "row_done",
                                                                     "row_added", "rows_out")
    c_loaded, zeroed, bias_loaded, rows_loaded = g.sems("m", "c_loaded", "zeroed", "bias_loaded", "rows_loaded")
    first_rows_out = g.sem("first_rows_out")
    slab_loaded = [g.sem(f"slab_loaded_m{r}") for r in range(SLABS)]
    with ExitStack() as s:
        sb = lambda n, shape: s.enter_context(nc.sbuf_tensor(n, shape, F32))
        slab = sb("mod_slab", [P, SLABS, KD, 512])
        c = sb("c_cols", [P, KD, 2])
        e = sb("c_exp", [P, KD, 2])
        bias = sb("mod_bias", [2, DEPTH * 6 * D])
        rows = sb("mod_out", [2, DEPTH * 6 * D])
        with nc.Block() as block:
            @block.sync
            def _(sp):
                with nc.allow_non_contiguous_dma(reason="a vector onto partitions"):
                    sp.dma_start(c[:, :, 0], a["c"].rearrange("b (k p) -> p (b k)", p=P)).then_inc(c_loaded, 16)
                    sp.dma_start(c[:, :, 1], a["c_ctx"].rearrange("(k p) -> p k", p=P)).then_inc(c_loaded, 16)
                sp.dma_start(bias[:], a["b_mod"].rearrange("l n -> (l n)").partition_broadcast(2)).then_inc(bias_loaded, 16)
                for l in range(DEPTH):
                    w = a["w_mod"][l].rearrange("(k p) n -> p k n", p=P)
                    with sp.Fori(0, NCH // SLABS) as i:
                        for r in range(SLABS):
                            sp.wait_ge(row_done, i * SLABS + (l * NCH + r + 1))
                            sp.dma_start(slab[:, r], w[:, :, bass.ds(i * (SLABS * 512) + r * 512, 512)]
                                         ).then_inc(slab_loaded[r], 16)
                    if l == 0:
                        sp.dma_start(g.x[:, 0:NX], a["x"].rearrange("b (t p) d -> p (b t) d", p=P)
                                     ).then_inc(tensors_loaded, 16)
                        sp.dma_start(g.x[:, NX:], a["ctx"].rearrange("b (t p) d -> p (b t) d", p=P)
                                     ).then_inc(tensors_loaded, 16)
                        sp.dma_start(g.ident[:], a["identity"]).then_inc(tensors_loaded, 16)
                        sp.dma_start(g.rope[NOPE:], a["rope_tables"]).then_inc(tensors_loaded, 16)
                sp.wait_ge(row_added, DEPTH * NCH + SLABS)
                for l in range(1, DEPTH):
                    at = slice(l * 6 * D, (l + 1) * 6 * D)
                    sp.dma_start(g.mod_dram[:, at], rows[:, at]).then_inc(rows_out, 16)
                sp.wait_ge(rows_out, 16 * (DEPTH - 1))
                sp.wait_ge(tensors_loaded, 64)

            @block.gpsimd
            def _(pool):
                pool.memset(g.ones[:], 1.0)
                pool.memset(g.half[:], -0.5)
                pool.iota(g.iota[:], [[1, TOPK]], base=0, channel_multiplier=0,
                          allow_small_or_imprecise_dtypes=True)

            @block.scalar
            def _(act):
                act.wait_ge(c_loaded, 32)
                act.activation(e[:], c[:], ACT.Exp, scale=-1.0).then_inc(zeroed, 1)
                act.wait_ge(row_added, NCH + SLABS)
                act.dma_start(g.mod_dram[:, 0:6 * D], rows[:, 0:6 * D]).then_inc(first_rows_out, 16)
                act.wait_ge(first_rows_out, 16)
                load_mod_rows(g, act, 0, 0, range(0, 2), rows_loaded)
                act.wait_ge(rows_loaded, 32)

            @block.vector
            def _(dve):
                link = Links(dve, g.dve_step)
                dve.sem_inc(row_added, SLABS)
                dve.wait_ge(zeroed, 1)
                link(dve.tensor_scalar(e[:], e[:], 1.0, None, ALU.add))
                link(dve.reciprocal(e[:], e[:]))
                dve.tensor_tensor(c[:], c[:], e[:], ALU.mult).then_inc(c_ready, 1)
                dve.wait_ge(bias_loaded, 16)
                for l in range(DEPTH):
                    with dve.Fori(0, NCH // SLABS) as i:
                        for r in range(SLABS):
                            at = bass.ds(i * (SLABS * 512) + (l * NCH + r) * 512, 512)
                            dve.wait_ge(row_done, i * SLABS + (l * NCH + r + 1 + SLABS))
                            dve.tensor_tensor(rows[:, at], g.ps[0:2, r, :], bias[:, at], ALU.add).then_inc(row_added, 1)
                link.reset()

            @block.tensor
            def _(pe):
                pe.sem_inc(row_done, SLABS)
                pe.wait_ge(c_ready, 1)
                for l in range(DEPTH):
                    with pe.Fori(0, NCH // SLABS) as i:
                        for r in range(SLABS):
                            pe.wait_ge(slab_loaded[r], i * 16 + 16 * (l * NCH // SLABS + 1))
                            pe.wait_ge(row_added, i * SLABS + (l * NCH + r + 1))
                            for k in range(KD):
                                last = pe.matmul(g.ps[0:2, r, :], c[:, k, :], slab[:, r, k, :],
                                                 start=(k == 0), stop=(k == KD - 1))
                            last.then_inc(row_done, 1)


@phase
def norm_and_project(g, l, which, tiles, h, out):
    nc, a = g.nc, g.a
    tag = f"{l}{which}"
    rows_loaded, squared, mean_ready, rstd_ready, h_ready, transposed, ht_ready, chunk_done, chunk_copied = g.sems(
        tag, "rows_loaded", "squared", "mean_ready", "rstd_ready", "h_ready", "transposed", "ht_ready",
        "chunk_done", "chunk_copied")
    keys_loaded, gates_loaded, cols_loaded = g.sems(tag, "keys_loaded", "gates_loaded", "cols_loaded")
    slab_loaded = [g.sem(f"slab_loaded_{tag}{r}") for r in range(2)]
    if which == 0:
        w = a["w_in"][l].rearrange("(k p) n -> p k n", p=P)
    norm_g = (a["norm1_g"] if which == 0 else a["norm2_g"])[l]
    looped = 12
    tokens = tiles * P
    wide = SEQ if which == 0 and l == DEPTH - 1 else tokens
    with ExitStack() as s:
        sb = lambda n, shape: s.enter_context(nc.sbuf_tensor(f"{n}_{tag}", shape, F32))
        grow = sb("norm_g_row", [P, D])
        ht = out["h_t"]
        slab = out["slab"]
        stat = sb("stat", [P, 3, NT])
        if which == 0:
            kr_rot = sb("kr_rot", [P, SEQ])

        parts = ((0, FIRST), (FIRST, tiles))

        def stream(t):
            return 0 if t < NX else 1

        with nc.Block() as block:
            @block.sync
            def _(sp):
                if which == 0 and l > 0:
                    load_mod_rows(g, sp, l, 0, range(0, 2), rows_loaded)
                sp.dma_start(grow[:], norm_g.partition_broadcast(P)).then_inc(rows_loaded, 16)
                if which == 1:
                    for r in range(2):
                        sp.dma_start(slab[:, r], a["peer_w_q"][l, r]).then_inc(slab_loaded[r], 16)
                    sp.dma_start(out["keys_t"][:], a["peer_sub_keys"][l]).then_inc(keys_loaded, 16)
                    load_mod_rows(g, sp, l, 1, range(2, 3), gates_loaded)
                    sp.wait_ge(keys_loaded, 16)
                else:
                    with sp.Fori(0, looped // 2) as i:
                        for r in range(2):
                            sp.wait_ge(chunk_done, i * 2 + (r + 1))
                            sp.dma_start(slab[:, r], w[:, :, bass.ds(i * (2 * P) + r * P, P)]).then_inc(slab_loaded[r], 16)
                    sp.wait_ge(chunk_done, looped + 1)
                    sp.dma_start(slab[:, 0], w[:, :, KVCHUNK * P:(KVCHUNK + 1) * P]).then_inc(slab_loaded[0], 16)
                    load_mod_rows(g, sp, l, 0, range(2, 3), gates_loaded)
                    sp.wait_ge(chunk_done, looped + 2)
                    sp.dma_start(slab[:, 1], w[:, :, KRCHUNK * P - NOPE:]).then_inc(slab_loaded[1], 16)
                    with nc.allow_non_contiguous_dma(reason="vectors onto partitions"):
                        col = lambda name: a[name][l].rearrange("(c p) -> p c", p=P)
                        sp.dma_start(g.cols[:, :, 34], col("conv_b_bias")).then_inc(cols_loaded, 16)
                        sp.dma_start(g.cols[:, :, 35], col("conv_b_ln_g")).then_inc(cols_loaded, 16)
                        sp.dma_start(g.cols[:, :, 36], col("conv_b_ln_b")).then_inc(cols_loaded, 16)
                        sp.dma_start(g.cols[:, :, 37], col("mla_q_norm_g")).then_inc(cols_loaded, 16)
                        sp.dma_start(g.kvg[:], col("mla_kv_norm_g")).then_inc(cols_loaded, 16)
                        for c in range(2):
                            sp.dma_start(g.cols[:, c, 0:CONV_A], a["conv_a_w"][l][:, c * P:(c + 1) * P].rearrange(
                                "k p -> p k")).then_inc(cols_loaded, 16)
                            sp.dma_start(g.cols[:, c, CONV_A:CONV_A + CONV_B], a["conv_b_w"][l][:, c * P:(c + 1) * P].rearrange(
                                "k p -> p k")).then_inc(cols_loaded, 16)
                    sp.wait_ge(cols_loaded, 16 * 9)
                sp.wait_ge(gates_loaded, 32)

            @block.scalar
            def _(act):
                act.sem_inc(chunk_copied, 2)
                for t in range(tiles):
                    act.activation(h[:, t], g.x[:, t], ACT.Square, accum_out=stat[:, 0, t:t + 1]).then_inc(squared, 1)
                for t in range(tiles):
                    if which == 1 and t == FIRST:
                        for c in range(2):
                            act.wait_ge(chunk_done, c + 3)
                            act.activation(out["proj"][:, c, 0:FIRST * P], g.psum2(2 + c)[:, 0:FIRST * P], ACT.Copy)
                    act.wait_ge(transposed, t + 1)
                    act.activation(ht[:, :, t * P:(t + 1) * P], g.psum2(t % 2).rearrange("p (k n) -> p k n", k=KD),
                                   ACT.Copy).then_inc(ht_ready, 1)
                if which == 1:
                    return
                with act.Fori(0, looped // 2) as i:
                    for r in range(2):
                        act.wait_ge(chunk_done, i * 2 + (r + 3))
                        act.activation(out["proj"][:, bass.ds(i * 2 + r, 1), 0:wide].rearrange("p c n -> p (c n)"),
                                       g.psum2(r)[:, 0:wide], ACT.Copy).then_inc(chunk_copied, 1)
                act.wait_ge(chunk_done, looped + 3)
                act.activation(out["proj"][:, KVCHUNK], g.psum2(0)[:, 0:TOK], ACT.Copy).then_inc(chunk_copied, 1)

            @block.gpsimd
            def _(pool):
                for n, (lo, hi) in enumerate(parts):
                    pool.wait_ge(mean_ready, n + 1)
                    pool.tensor_tensor(stat[:, 2, lo:hi], stat[:, 1, lo:hi], g.half[:, lo:hi], ALU.pow).then_inc(rstd_ready, 1)

            @block.vector
            def _(dve):
                link = Links(dve, g.dve_step)
                for n, (lo, hi) in enumerate(parts):
                    dve.wait_ge(squared, hi)
                    dve.tensor_scalar(stat[:, 1, lo:hi], stat[:, 0, lo:hi], 1.0 / D, EPS, ALU.mult, ALU.add
                                      ).then_inc(mean_ready, 1)
                    if n == 0:
                        dve.wait_ge(rows_loaded, 48 if which == 0 and l > 0 else 16)
                    for t in range(lo, hi):
                        if t in (0, NX):
                            scale = g.rows[:, stream(t), 1]
                            link(dve.scalar_tensor_tensor(scale, scale, 1.0, grow[:], ALU.add, ALU.mult))
                        dve.wait_ge(rstd_ready, n + 1)
                        link(dve.scalar_tensor_tensor(h[:, t], g.x[:, t], stat[:, 2, t:t + 1], scale, ALU.mult, ALU.mult))
                        dve.tensor_tensor(h[:, t], h[:, t], g.rows[:, stream(t), 0], ALU.add).then_inc(h_ready, 1)
                if which == 0:
                    dve.wait_ge(chunk_done, looped + 4)
                    kr, turned, kt = slice(NOPE, QK), slice(QK, P), out["k_t"]
                    link(dve.tensor_tensor(kr_rot[kr], g.psum2(1)[turned, 0:SEQ], g.rope[turned], ALU.mult))
                    for e in range(2):
                        link.mark(dve.tensor_copy(kt[kr, e, SEQ:], g.psum2(1)[kr, SEQ:TOK]))
                        link(dve.tensor_tensor(kt[kr, e, 0:SEQ], g.psum2(1)[kr, 0:SEQ], g.rope[kr], ALU.mult))
                        link(dve.tensor_tensor(kt[kr, e, 0:SEQ], kt[kr, e, 0:SEQ], kr_rot[kr], ALU.add))
                link.reset()

            @block.tensor
            def _(pe):
                pe.sem_inc(chunk_done, 2)

                def chunk(psum, lhs, m, n_tok):
                    for k in range(KD):
                        for at in range(0, n_tok, 512):
                            to = min(at + 512, n_tok)
                            last = pe.matmul(psum[0:m, at:to], lhs[:, k, 0:m], ht[:, k, at:to],
                                             start=(k == 0), stop=(k == KD - 1))
                    last.then_inc(chunk_done, 1)

                for t in range(tiles):
                    pe.wait_ge(h_ready, t + 1)
                    if t >= 2:
                        pe.wait_ge(ht_ready, t - 1)
                    for k in range(KD):
                        last = pe.transpose(g.psum2(t % 2)[:, k * P:(k + 1) * P], h[:, t, k * P:(k + 1) * P], g.ident[:])
                    last.then_inc(transposed, 1)
                    if which == 1 and t == FIRST - 1:
                        pe.wait_ge(ht_ready, FIRST)
                        for c in range(2):
                            pe.wait_ge(slab_loaded[c], 16)
                            chunk(g.psum2(2 + c), slab[:, c], P, FIRST * P)
                if which == 1:
                    return
                pe.wait_ge(ht_ready, tiles)
                with pe.Fori(0, looped // 2) as i:
                    for r in range(2):
                        pe.wait_ge(slab_loaded[r], i * 16 + 16)
                        pe.wait_ge(chunk_copied, i * 2 + (r + 1))
                        chunk(g.psum2(r), slab[:, r], P, wide)
                pe.wait_ge(slab_loaded[0], 16 * (looped // 2 + 1))
                pe.wait_ge(chunk_copied, looped + 1)
                chunk(g.psum2(0), slab[:, 0], P, TOK)
                pe.wait_ge(slab_loaded[1], 16 * (looped // 2 + 1))
                pe.wait_ge(chunk_copied, looped + 2)
                chunk(g.psum2(1), slab[:, 1], P, TOK)


@phase
def mix(g, l, proj, k_t, cat):
    nc, a = g.nc, g.a
    tag = f"{l}x"
    last_layer = l == DEPTH - 1
    tiles = NX if last_layer else NT
    W = tiles * P
    WA = W if last_layer else W + PAD_A
    WB = W if last_layer else W + PAD_B
    latent_squared, latent_summed, latent_mean, latent_root, latent_ready = g.sems(
        tag, "latent_squared", "latent_summed", "latent_mean", "latent_root", "latent_ready")
    v_done, v_copied, kv_loaded, padded, sigmoid_ready = g.sems(tag, "v_done", "v_copied", "kv_loaded", "padded", "sigmoid_ready")
    q_done, k_done, qk_copied, rope_done = g.sems(tag, "q_done", "k_done", "qk_copied", "rope_done")
    logged, conv_activated, tile_done, tile_scaled, rows_loaded = g.sems(
        tag, "logged", "conv_activated", "tile_done", "tile_scaled", "rows_loaded")
    w_loaded = [g.sem(f"w_out_loaded_{tag}{k}") for k in range(KD)]
    scored, shift_ready, exp_done, p_turned, pt_copied, pv_done, o_ready = g.sems(
        tag, "scored", "shift_ready", "exp_done", "p_turned", "pt_copied", "pv_done", "o_ready")
    conv_ready, conv_sum, conv_centred, conv_squared, conv_var, conv_root, conv_scaled = g.sems(
        tag, "conv_ready", "conv_sum", "conv_centred", "conv_squared", "conv_var", "conv_root", "conv_scaled")
    head_loaded = [g.sem(f"head_loaded_{tag}{e}") for e in range(2)]
    with ExitStack() as s:
        sb = lambda n, shape: s.enter_context(nc.sbuf_tensor(f"{n}_{tag}", shape, F32))
        wkv = sb("w_ukv", [P, HEADS, NOPE + VD])
        wq_head = sb("w_uq_head", [P, 2, 2, P])
        wk_head = sb("w_uk_head", [P, 2, NOPE])
        v = sb("v", [P, NT, HEADS * VD])
        q_t = sb("q_t", [P, 2, W])
        rot = sb("q_rot", [P, SEQ])
        prob = sb("prob", [P, 2, TOK])
        prob_t = sb("prob_t", [P, 2, TOK])
        o = sb("o", [P, tiles, 2 * VD])
        soft = sb("soft", [P, 4, 2 * NT])
        z_a = sb("z_a", [P, 2, TOK + 3 * PAD_A])
        z_b = sb("z_b", [P, 2, TOK + 3 * PAD_B])
        acc_b = sb("acc_b", [P, 2, TOK + PAD_B])
        work = sb("work", [P, 3, TOK + PAD_B])
        rstd = sb("rstd", [P, 2, TOK])
        newton = sb("newton", [P, TOK])
        w_last = sb("w_out_last", [P, D])
        proj_flat = proj[:].rearrange("p c n -> p (c n)")
        w_out = [proj_flat[:, k * D:(k + 1) * D] for k in range(KD - 1)] + [w_last[:]]
        scaled = z_a[:].rearrange("p c n -> p (c n)")[:, 0:D]
        out_bank = (3, 2, 0, 1)
        last_taps = range(CONV_B - 2, CONV_B)
        PER_PAIR = (CONV_B - 3) // (HEADS // 2)
        per_pair_tiles = 2 * tiles
        turned_per_pair = per_pair_tiles + 1

        def streams(pad):
            yield slice(0, SEQ), slice(pad, pad + SEQ)
            if not last_layer:
                yield slice(SEQ, TOK), slice(2 * pad + SEQ, 2 * pad + TOK)

        def key_range(u):
            return (0, TOK) if u < NX else (SEQ, TOK)

        with nc.Block() as block:
            @block.sync
            def _(sp):
                sp.dma_start(wkv[:], a["w_ukv"][l].rearrange("p (h n) -> p h n", h=HEADS)).then_inc(kv_loaded, 16)
                wq = a["w_uq"][l].rearrange("(k p) n -> p k n", p=P)
                wk = a["w_ukv"][l]
                with sp.Fori(0, HEADS // 2) as i:
                    for e in range(2):
                        sp.wait_ge(k_done, i * 2 + (e + 1))
                        sp.dma_start(wq_head[:, e], wq[:, :, bass.ds(i * (2 * P) + e * P, P)]).then_inc(head_loaded[e], 16)
                        sp.dma_start(wk_head[:, e], wk[:, bass.ds(i * (2 * P) + e * P, NOPE)]).then_inc(head_loaded[e], 16)
                sp.wait_ge(rope_done, 1)
                for k in range(KD):
                    sp.dma_start(w_out[k], a["w_out"][l, k * P:(k + 1) * P]).then_inc(w_loaded[k], 16)
                load_mod_rows(g, sp, l, 1, range(0, 2), rows_loaded)
                sp.wait_ge(rows_loaded, 32)

            @block.gpsimd
            def _(pool):
                pool.memset(z_a[:], 0.0).then_inc(padded, 1)
                pool.memset(z_b[:], 0.0).then_inc(padded, 1)

            @block.scalar
            def _(act):
                act.sem_inc(pt_copied, 1)
                act.sem_inc(exp_done, 1)
                act.activation(work[:, 2, 0:TOK], proj[:, KVCHUNK], ACT.Square).then_inc(latent_squared, 1)
                act.activation(work[:, 0:2, 0:W], proj[:, QCHUNK:QCHUNK + 2, 0:W], ACT.Square).then_inc(latent_squared, 1)
                def first_rstd(i, at, w_, n, done):
                    act.activation(rstd[:, i, 0:w_], work[:, at, 0:w_], ACT.Ln).then_inc(logged, 1)
                    act.wait_ge(logged, n)
                    act.activation(rstd[:, i, 0:w_], rstd[:, i, 0:w_], ACT.Exp, scale=-0.5).then_inc(done, 1)

                for n, (i, at, w_) in enumerate(((1, 2, TOK), (0, 0, W))):
                    act.wait_ge(latent_mean, n + 1)
                    first_rstd(i, at, w_, n + 1, latent_root)
                act.activation(proj[:, 8:10, 0:W], proj[:, 8:10, 0:W], ACT.Sigmoid).then_inc(sigmoid_ready, 1)
                for t in range(NT):
                    act.wait_ge(v_done, t + 1)
                    act.activation(v[:, t], g.ps[:, 4 + t % 2], ACT.Copy).then_inc(v_copied, 1)
                with act.Fori(0, HEADS // 2) as i:
                    for e in range(2):
                        act.wait_ge(q_done, i * 2 + (e + 1))
                        act.activation(q_t[0:NOPE, e], g.psum2(0)[0:NOPE, 0:W], ACT.Copy).then_inc(qk_copied, 1)
                        if not last_layer:
                            act.activation(q_t[NOPE:QK, e, SEQ:], g.psum2(0)[NOPE:QK, SEQ:TOK], ACT.Copy).then_inc(qk_copied, 1)
                        act.wait_ge(k_done, i * 2 + (e + 3))
                        act.activation(k_t[0:NOPE, e], g.psum2(1)[0:NOPE, 0:TOK], ACT.Copy).then_inc(qk_copied, 1)
                        for u in range(tiles):
                            lo, hi = key_range(u)
                            n = e * tiles + u
                            act.wait_ge(shift_ready, i * per_pair_tiles + (n + 1))
                            act.activation(prob[:, n % 2, lo:hi], g.psum2(n % 2)[:, lo:hi], ACT.Exp, scale=SCALE,
                                           bias=soft[:, 1, n:n + 1], accum_out=soft[:, 2, n:n + 1]).then_inc(exp_done, 1)
                            act.wait_ge(p_turned, i * turned_per_pair + (n + 1))
                            act.activation(prob_t[:, n % 2, lo:hi], g.psum2(2)[:, lo:hi], ACT.Copy).then_inc(pt_copied, 1)
                    act.wait_ge(p_turned, i * turned_per_pair + turned_per_pair)
                    act.activation(cat[:, bass.ds(i + 4, 1), 0:W].rearrange("p c n -> p (c n)"), g.psum2(2)[:, 0:W],
                                   ACT.Copy).then_inc(pt_copied, 1)
                act.wait_ge(conv_centred, 1)
                act.activation(work[:, 0:2, 0:W], acc_b[:, :, 0:W], ACT.Square).then_inc(conv_squared, 1)
                act.wait_ge(conv_var, 1)
                first_rstd(0, 2, W, 3, conv_root)
                for c in range(2):
                    act.wait_ge(conv_scaled, c + 1)
                    act.activation(cat[:, 2 + c, 0:W], cat[:, 2 + c, 0:W], ACT.Silu, scale=g.cols[:, c, 35:36],
                                   bias=g.cols[:, c, 36:37]).then_inc(conv_activated, 1)

            @block.vector
            def _(dve):
                link = Links(dve, g.dve_step)
                dve.wait_ge(latent_summed, 1)
                dve.tensor_scalar(work[:, 2, 0:TOK], g.psum2(1)[:, 0:TOK], 1.0 / P, EPS, ALU.mult, ALU.add).then_inc(latent_mean, 1)
                dve.wait_ge(latent_summed, 2)
                dve.tensor_scalar(work[:, 0, 0:W], g.psum2(0)[:, 0:W], 1.0 / (2 * P), EPS, ALU.mult, ALU.add).then_inc(latent_mean, 1)

                def refined_rstd(i, at, w_):
                    y, t, v_ = rstd[:, i, 0:w_], newton[:, 0:w_], work[:, at, 0:w_]
                    link(dve.tensor_tensor(t, y, y, ALU.mult))
                    link(dve.tensor_tensor(t, t, v_, ALU.mult))
                    link(dve.tensor_scalar(t, t, -0.5, 1.5, ALU.mult, ALU.add))
                    link(dve.tensor_tensor(y, y, t, ALU.mult))

                dve.wait_ge(latent_root, 1)
                refined_rstd(1, 2, TOK)
                dve.scalar_tensor_tensor(proj[:, KVCHUNK], proj[:, KVCHUNK], g.kvg[:, 0:1], rstd[:, 1], ALU.mult,
                                         ALU.mult).then_inc(latent_ready, 1)
                dve.wait_ge(latent_root, 2)
                refined_rstd(0, 0, W)
                for c in range(2):
                    dve.scalar_tensor_tensor(proj[:, QCHUNK + c, 0:W], proj[:, QCHUNK + c, 0:W], g.cols[:, c, 37:38],
                                             rstd[:, 0, 0:W], ALU.mult, ALU.mult).then_inc(latent_ready, 1)
                dve.wait_ge(padded, 2)
                dve.wait_ge(sigmoid_ready, 1)
                for tok, at in streams(PAD_A):
                    link.mark(dve.tensor_tensor(z_a[:, :, at], proj[:, 2:4, tok], proj[:, 4:6, tok], ALU.mult))
                for tok, at in streams(PAD_B):
                    link.mark(dve.tensor_tensor(z_b[:, :, at], proj[:, 6:8, tok], proj[:, 8:10, tok], ALU.mult))
                link.wait()
                acc_a = work[:, 1:3, 0:WA]
                for c in range(2):
                    link.mark(dve.tensor_scalar(acc_a[:, c], z_a[:, c, 0:WA], g.cols[:, c, 0:1], None, ALU.mult))
                for k in range(1, CONV_A):
                    for c in range(2):
                        link.wait(1)
                        link.mark(dve.scalar_tensor_tensor(acc_a[:, c], z_a[:, c, k:k + WA], g.cols[:, c, k:k + 1],
                                                           acc_a[:, c], ALU.mult, ALU.add))
                link.wait()
                for tok, at in streams(PAD_A):
                    out_at = slice(at.start - PAD_A, at.stop - PAD_A)
                    link.mark(dve.tensor_tensor(cat[:, 0:2, tok], proj[:, 0:2, tok], acc_a[:, :, out_at], ALU.mult))

                def tap(k, c):
                    link.wait(1)
                    at = bass.ds(k, WB)
                    w_at = bass.ds(k + CONV_A, 1)
                    link.mark(dve.scalar_tensor_tensor(acc_b[:, c, 0:WB], z_b[:, c, at], g.cols[:, c, w_at],
                                                       acc_b[:, c, 0:WB], ALU.mult, ALU.add))

                for c in range(2):
                    link.mark(dve.tensor_scalar(acc_b[:, c, 0:WB], z_b[:, c, 0:WB], g.cols[:, c, CONV_A:CONV_A + 1],
                                                g.cols[:, c, 34:35], ALU.mult, ALU.add))
                link.reset()
                rp, turned = slice(NOPE, QK), slice(QK, P)
                with dve.Fori(0, HEADS // 2) as i:
                    todo = [(k, c) for k in range(PER_PAIR) for c in range(2)]
                    total = len(todo)

                    def o_part(n):
                        e, u = divmod(n, tiles)
                        dve.wait_ge(pv_done, i * per_pair_tiles + (n + 1))
                        link(dve.reciprocal(soft[:, 3, n:n + 1], soft[:, 2, n:n + 1]))
                        dve.tensor_scalar(o[:, u, e * VD:(e + 1) * VD], g.ps[:, 6 + n % 2, 0:VD],
                                          soft[:, 3, n:n + 1], None, ALU.mult).then_inc(o_ready, 1)

                    for e in range(2):
                        dve.wait_ge(q_done, i * 2 + (e + 1))
                        link.mark(dve.tensor_tensor(rot[rp], g.psum2(0)[turned, 0:SEQ], g.rope[turned], ALU.mult))
                        link(dve.tensor_tensor(q_t[rp, e, 0:SEQ], g.psum2(0)[rp, 0:SEQ], g.rope[rp], ALU.mult))
                        dve.tensor_tensor(q_t[rp, e, 0:SEQ], q_t[rp, e, 0:SEQ], rot[rp], ALU.add).then_inc(rope_done, 1)
                        for u in range(tiles):
                            lo, hi = key_range(u)
                            n = e * tiles + u
                            dve.wait_ge(scored, i * per_pair_tiles + (n + 1))
                            link(dve.tensor_reduce(soft[:, 0, n:n + 1], g.psum2(n % 2)[:, lo:hi], AX_X, ALU.max))
                            dve.tensor_scalar(soft[:, 1, n:n + 1], soft[:, 0, n:n + 1], -SCALE, None, ALU.mult
                                              ).then_inc(shift_ready, 1)
                            while total - len(todo) < (n + 1) * total // per_pair_tiles:
                                k, c = todo.pop(0)
                                tap(i * PER_PAIR + (1 + k), c)
                            if u >= 2:
                                o_part(n - 2)
                        o_part(n - 1)
                        o_part(n)
                    link.reset()
                for k in last_taps:
                    for c in range(2):
                        tap(k, c)
                link.wait()
                dve.tensor_copy(acc_b[:, 0, 0:1], acc_b[:, 0, 0:1]).then_inc(conv_ready, 1)
                dve.wait_ge(conv_sum, 1)
                link(dve.tensor_scalar(work[:, 2, 0:W], g.psum2(0)[:, 0:W], 1.0 / (2 * P), None, ALU.mult))
                for c in range(2):
                    for tok, at in streams(PAD_B):
                        out_at = slice(at.start - PAD_B, at.stop - PAD_B)
                        link(dve.tensor_tensor(cat[:, 2 + c, tok], acc_b[:, c, out_at], work[:, 2, tok], ALU.subtract))
                dve.tensor_copy(acc_b[:, :, 0:W], cat[:, 2:4, 0:W]).then_inc(conv_centred, 1)
                dve.wait_ge(conv_sum, 2)
                dve.tensor_scalar(work[:, 2, 0:W], g.psum2(1)[:, 0:W], 1.0 / (2 * P), EPS, ALU.mult, ALU.add).then_inc(conv_var, 1)
                dve.wait_ge(conv_root, 1)
                refined_rstd(0, 2, W)
                for c in range(2):
                    dve.tensor_tensor(cat[:, 2 + c, 0:W], cat[:, 2 + c, 0:W], rstd[:, 0, 0:W], ALU.mult).then_inc(conv_scaled, 1)
                for t in range(tiles):
                    dve.wait_ge(tile_done, t + 1)
                    dve.tensor_tensor(scaled, g.psum2(out_bank[t % 4]), g.rows[:, 0 if t < NX else 1, 2], ALU.mult
                                      ).then_inc(tile_scaled, 1)
                    dve.wait_ge(tile_scaled, t + 1)
                    link(dve.tensor_tensor(g.x[:, t], g.x[:, t], scaled, ALU.add))
                link.reset()

            @block.tensor
            def _(pe):
                def spans(n_tok):
                    return [(at, min(at + 512, n_tok)) for at in range(0, n_tok, 512)]

                pe.sem_inc(k_done, 2)
                pe.wait_ge(latent_squared, 1)
                for lo, hi in spans(TOK):
                    last = pe.matmul(g.psum2(1)[:, lo:hi], g.ones[:], work[:, 2, lo:hi], start=True, stop=True)
                last.then_inc(latent_summed, 1)
                pe.wait_ge(latent_squared, 2)
                for c in range(2):
                    for lo, hi in spans(W):
                        last = pe.matmul(g.psum2(0)[:, lo:hi], g.ones[:], work[:, c, lo:hi], start=(c == 0), stop=(c == 1))
                last.then_inc(latent_summed, 1)
                pe.wait_ge(latent_ready, 1)
                pe.wait_ge(kv_loaded, 16)
                for t in range(NT):
                    if t >= 2:
                        pe.wait_ge(v_copied, t - 1)
                    pe.matmul(g.ps[:, 4 + t % 2], proj[:, KVCHUNK, t * P:(t + 1) * P], wkv[:, :, NOPE:],
                              start=True, stop=True).then_inc(v_done, 1)
                pe.wait_ge(v_copied, NT)
                pe.wait_ge(latent_ready, 3)
                with pe.Fori(0, HEADS // 2) as i:
                    copies = 2 if last_layer else 3
                    for e in range(2):
                        n0 = e * tiles
                        pe.wait_ge(head_loaded[e], i * 32 + 32)
                        pe.wait_ge(exp_done, i * per_pair_tiles + (n0 + 1))
                        for k in range(2):
                            for lo, hi in spans(W):
                                last = pe.matmul(g.psum2(0)[:, lo:hi], wq_head[:, e, k, :], proj[:, QCHUNK + k, lo:hi],
                                                 start=(k == 0), stop=(k == 1))
                        last.then_inc(q_done, 1)
                        for lo, hi in spans(TOK):
                            last = pe.matmul(g.psum2(1)[0:NOPE, lo:hi], wk_head[:, e, :], proj[:, KVCHUNK, lo:hi],
                                             start=True, stop=True)
                        last.then_inc(k_done, 1)
                        pe.wait_ge(qk_copied, i * (2 * copies) + copies * (e + 1))
                        pe.wait_ge(rope_done, i * 2 + (e + 1))

                        def score(u):
                            n = n0 + u
                            if u >= 2:
                                pe.wait_ge(exp_done, i * per_pair_tiles + n)
                            lo, hi = key_range(u)
                            for at in range(lo, hi, 512):
                                to = min(at + 512, hi)
                                last = pe.matmul(g.psum2(n % 2)[:, at:to], q_t[0:QK, e, u * P:(u + 1) * P],
                                                 k_t[0:QK, e, at:to], start=True, stop=True)
                            last.then_inc(scored, 1)

                        def turn(u):
                            n = n0 + u
                            lo, hi = key_range(u)
                            pe.wait_ge(exp_done, i * per_pair_tiles + (n + 2))
                            pe.wait_ge(pt_copied, i * turned_per_pair + (n + 1))
                            for at in range(lo, hi, P):
                                last = pe.transpose(g.psum2(2)[:, at:at + P], prob[:, n % 2, at:at + P], g.ident[:])
                            last.then_inc(p_turned, 1)

                        def weigh(u):
                            n = n0 + u
                            lo, hi = key_range(u)
                            pe.wait_ge(pt_copied, i * turned_per_pair + (n + 2))
                            if n >= 2:
                                pe.wait_ge(o_ready, i * per_pair_tiles + (n - 1))
                            for at in range(lo, hi, P):
                                last = pe.matmul(g.ps[:, 6 + n % 2, 0:VD], prob_t[:, n % 2, at:at + P],
                                                 v[:, at // P, bass.ds(i * (2 * VD) + e * VD, VD)],
                                                 start=(at == lo), stop=(at + P == hi))
                            last.then_inc(pv_done, 1)

                        score(0)
                        for u in range(tiles):
                            if u + 1 < tiles:
                                score(u + 1)
                            if u >= 1:
                                weigh(u - 1)
                            turn(u)
                        weigh(tiles - 1)
                    pe.wait_ge(o_ready, i * per_pair_tiles + per_pair_tiles)
                    for u in range(tiles):
                        last = pe.transpose(g.psum2(2)[:, u * P:(u + 1) * P], o[:, u, :], g.ident[:])
                    last.then_inc(p_turned, 1)
                def project_out(t, chunks, start, stop):
                    for k in chunks:
                        if t == 0:
                            pe.wait_ge(w_loaded[k], 16)
                        for b in range(2):
                            last = pe.matmul(g.psum2(out_bank[t % 4])[:, b * 512:(b + 1) * 512], cat[:, k, t * P:(t + 1) * P],
                                             w_out[k][:, b * 512:(b + 1) * 512], start=(start and k == chunks[0]),
                                             stop=(stop and k == chunks[-1]))
                    if stop:
                        last.then_inc(tile_done, 1)

                at_once, later = [0, 1, 4, 5, 6, 7], [2, 3]
                pe.wait_ge(pt_copied, HEADS // 2 * turned_per_pair + 1)
                project_out(0, at_once, True, False)
                pe.wait_ge(conv_ready, 1)
                for c in range(2):
                    for tok, at in streams(PAD_B):
                        out_at = slice(at.start - PAD_B, at.stop - PAD_B)
                        last = pe.matmul(g.psum2(0)[:, tok], g.ones[:], acc_b[:, c, out_at], start=(c == 0), stop=(c == 1))
                last.then_inc(conv_sum, 1)
                project_out(1, at_once, True, False)
                pe.wait_ge(conv_squared, 1)
                for c in range(2):
                    for lo, hi in spans(W):
                        last = pe.matmul(g.psum2(1)[:, lo:hi], g.ones[:], work[:, c, lo:hi], start=(c == 0), stop=(c == 1))
                last.then_inc(conv_sum, 1)
                project_out(2, at_once, True, False)
                pe.wait_ge(conv_activated, 2)
                for t in range(3):
                    project_out(t, later, False, True)
                for t in range(3, tiles):
                    if t >= 4:
                        pe.wait_ge(tile_scaled, t - 3)
                    project_out(t, at_once + later, True, True)


@phase
def peer(g, l, tiles, h, ht, slab, q_t, keys_t):
    nc, a = g.nc, g.a
    tag = f"{l}p"
    groups = tiles * PH
    (scored, ranked, idx_ready, best_ready, gate_ready, dotted, acted, weighted, diag_ready, v_used) = g.sems(tag, "scored", "ranked", "idx_ready", "best_ready", "gate_ready", "dotted",
                       "acted", "weighted", "diag_ready", "v_used")
    q_done, q_copied, summed = g.sems(tag, "q_done", "q_copied", "summed")
    slab_loaded = [g.sem(f"slab_loaded_{tag}{r}") for r in range(2)]
    u_loaded = [g.sem(f"u_loaded_{tag}{n}") for n in range(NU)]
    v_loaded = [g.sem(f"v_loaded_{tag}{n}") for n in range(NV)]
    NDIAG = 4
    rest = FIRST * P
    with ExitStack() as s:
        sb = lambda n, shape, dt=F32: s.enter_context(nc.sbuf_tensor(f"{n}_{tag}", shape, dt))
        u_buf = sb("u_rows", [P, NU, D])
        v_buf = sb("v_rows", [P, NV - 2, D])
        v_at = [v_buf[:, n] for n in range(NV - 2)] + [g.rows[:, 1, 0], g.rows[:, 1, 1]]
        scaled = g.rows[:, 0, 1]
        left = sb("left", [P, 2, P])
        top = sb("top", [P, 2, TOPK])
        top_i = sb("top_i", [P, 2, TOPK], U32)
        top_f = sb("top_f", [P, 2, TOPK])
        cand = sb("cand", [P, 2, TOPK * TOPK])
        best = sb("best", [P, 2, TOPK])
        best_i = sb("best_i", [P, TOPK], U32)
        pair_i = sb("pair_i", [P, 2, TOPK], U32)
        pair_f = sb("pair_f", [P, 2, TOPK])
        match = sb("match", [P, 2, TOPK, TOPK])
        found = sb("found", [P, 2, TOPK])
        shift = sb("shift", [P, 2, 1])
        total = sb("total", [P, 2, 2])
        idx = sb("idx", [P, tiles, TOPK], U32)
        gate = sb("gate", [P, 2, TOPK])
        dots = sb("dots", [P, 2, TOPK])
        gelu = sb("gelu", [P, 2, TOPK])
        wts = sb("wts", [P, 2, TOPK])
        diag = sb("diag", [P, NDIAG, P])

        def exists(b, k):
            return not isinstance(b, int) or b * tiles + k < groups

        def each_head(eng, body):
            with eng.Fori(0, PH - 1) as b:
                body(b)
            body(PH - 1)

        with nc.Block() as block:
            @block.sync
            def _(sp):
                with sp.Fori(0, PH - 1) as b:
                    for r in range(2):
                        sp.wait_ge(q_done, b * 2 + (r + 1))
                        sp.dma_start(slab[:, r], a["peer_w_q"][l, bass.ds(b * 2 + (r + 2), 1)].rearrange(
                            "c p k n -> p (c k) n")).then_inc(slab_loaded[r], 16)

            @block.gpsimd
            def _(pool):
                def gather(buf, table, k, j, loaded):
                    pool.nop(nofuse=True)
                    pool.indirect_dma_start(buf, None, table.rearrange("l e d -> (l e) d"),
                                            bass.IndirectOffsetOnAxis(idx[:, k % tiles, j:j + 1], 0),
                                            element_offset=l * NKEY * NKEY * D).then_inc(loaded, 16)

                pool.wait_ge(idx_ready, 1)
                for j in range(TOPK):
                    if j >= NU:
                        pool.wait_ge(dotted, j - NU + 1)
                    gather(u_buf[:, j % NU], a["peer_u"], 0, j, u_loaded[j % NU])

                def body(b):
                    for k in range(tiles):
                        with_u = exists(b, k + 1)
                        if with_u:
                            pool.wait_ge(idx_ready, b * tiles + (k + 2))
                        for j in range(TOPK):
                            if with_u:
                                pool.wait_ge(dotted, b * (tiles * TOPK) + ((k + 1) * TOPK + j - NU + 1))
                                gather(u_buf[:, j % NU], a["peer_u"], k + 1, j, u_loaded[j % NU])
                            pool.wait_ge(v_used, b * (tiles * TOPK) + (k * TOPK + j + 1))
                            gather(v_at[j % NV], a["peer_v"], k, j, v_loaded[j % NV])

                each_head(pool, body)

            @block.scalar
            def _(act):
                def gates(b, k):
                    if not exists(b, k):
                        return
                    act.wait_ge(best_ready, b * tiles + (k + 1))
                    act.activation(gate[:, k % 2], best[:, k % 2], ACT.Exp, bias=shift[:, k % 2],
                                   accum_out=total[:, k % 2, 0:1]).then_inc(gate_ready, 1)

                gates(0, 0)
                for c in range(2):
                    act.wait_ge(q_done, c + 1)
                    act.activation(q_t[:, c, rest:], g.psum2(2 + c)[:, rest:tiles * P], ACT.Copy).then_inc(q_copied, 1)

                def body(b):
                    for k in range(tiles):
                        if k == tiles - 2 and exists(b, tiles):
                            act.wait_ge(scored, b * tiles + tiles)
                            for c in range(2):
                                act.wait_ge(q_done, b * 2 + (c + 3))
                                act.activation(q_t[:, c], g.psum2(2 + c)[:, 0:tiles * P], ACT.Copy).then_inc(q_copied, 1)
                        gates(b, k + 1)
                        act.wait_ge(dotted, b * (tiles * TOPK) + (k + 1) * TOPK)
                        act.activation(gelu[:, k % 2], dots[:, k % 2], ACT.Gelu).then_inc(acted, 1)
                        act.wait_ge(weighted, b * tiles + (k + 1))
                        for j in range(TOPK):
                            act.wait_ge(v_used, b * (tiles * TOPK) + (k * TOPK + j + 1 - NDIAG + NV))
                            act.activation(diag[:, j % NDIAG], g.ident[:], ACT.Copy, scale=wts[:, k % 2, j:j + 1]
                                           ).then_inc(diag_ready, 1)

                each_head(act, body)

            @block.vector
            def _(dve):
                link = Links(dve, g.dve_step)

                def route(b, k):
                    if not exists(b, k):
                        return
                    r = k % 2
                    dve.wait_ge(scored, b * tiles + (k + 1))
                    dve.nop(nofuse=True)
                    for p in range(2):
                        sc = g.ps[:, r, p * P:(p + 1) * P]
                        link(dve.max(top[:, p, 0:8], sc))
                        link.mark(dve.max_index(top_i[:, p, 0:8], top[:, p, 0:8], sc))
                        link(dve.match_replace(left[:, p], top[:, p, 0:8], sc, LOWEST))
                        link(dve.max(top[:, p, 8:16], left[:, p]))
                        dve.max_index(top_i[:, p, 8:16], top[:, p, 8:16], left[:, p]).then_inc(ranked, 1)
                    dve.wait_ge(ranked, b * (2 * tiles) + (2 * k + 2))
                    link.mark(dve.tensor_tensor(cand[:, 0].rearrange("p (i j) -> p i j", i=TOPK),
                                                top[:, 0].unsqueeze(2).broadcast_to([P, TOPK, TOPK]),
                                                top[:, 1].unsqueeze(1).broadcast_to([P, TOPK, TOPK]), ALU.add))
                    link(dve.tensor_copy(top_f[:], top_i[:]))
                    link(dve.max(best[:, r, 0:8], cand[:, 0]))
                    link.mark(dve.max_index(best_i[:, 0:8], best[:, r, 0:8], cand[:, 0]))
                    link(dve.match_replace(cand[:, 1], best[:, r, 0:8], cand[:, 0], LOWEST))
                    link(dve.max(best[:, r, 8:16], cand[:, 1]))
                    link.mark(dve.max_index(best_i[:, 8:16], best[:, r, 8:16], cand[:, 1]))
                    dve.tensor_scalar(shift[:, r], best[:, r, 0:1], -1.0, None, ALU.mult).then_inc(best_ready, 1)
                    link.wait()
                    link.mark(dve.tensor_scalar(pair_i[:, 0], best_i[:], 4, None, ALU.logical_shift_right))
                    link(dve.tensor_scalar(pair_i[:, 1], best_i[:], TOPK - 1, None, ALU.bitwise_and))
                    link(dve.tensor_copy(pair_f[:], pair_i[:]))
                    for p in range(2):
                        link.mark(dve.tensor_tensor(match[:, p], pair_f[:, p].unsqueeze(2).broadcast_to([P, TOPK, TOPK]),
                                                    g.iota[:].unsqueeze(1).broadcast_to([P, TOPK, TOPK]), ALU.is_equal))
                    for p in range(2):
                        link.wait(1)
                        link.mark(dve.tensor_tensor(match[:, p], match[:, p],
                                                    top_f[:, p].unsqueeze(1).broadcast_to([P, TOPK, TOPK]), ALU.mult))
                    link.wait()
                    link(dve.tensor_reduce(found[:], match[:], AX_X, ALU.add))
                    dve.scalar_tensor_tensor(idx[:, k % tiles], found[:, 0], float(NKEY), found[:, 1], ALU.mult, ALU.add
                                             ).then_inc(idx_ready, 1)

                route(0, 0)
                link.reset()

                def body(b):
                    for k in range(tiles):
                        r = k % 2
                        route(b, k + 1)
                        for j in range(TOPK):
                            dve.wait_ge(u_loaded[j % NU], b * (16 * tiles * TOPK // NU) + 16 * ((k * TOPK + j) // NU + 1))
                            dve.tensor_tensor_reduce(u_buf[:, j % NU], u_buf[:, j % NU], h[:, k], 1.0, 0.0, ALU.mult,
                                                     ALU.add, dots[:, r, j:j + 1]).then_inc(dotted, 1)
                        dve.wait_ge(gate_ready, b * tiles + (k + 1))
                        link(dve.reciprocal(total[:, r, 1:2], total[:, r, 0:1]))
                        dve.wait_ge(acted, b * tiles + (k + 1))
                        dve.scalar_tensor_tensor(wts[:, r], gelu[:, r], total[:, r, 1:2], gate[:, r], ALU.mult, ALU.mult
                                                 ).then_inc(weighted, 1)
                        update(b, k)
                    link.reset()

                def update(b, k):
                    t = (k - 1) % tiles
                    dve.wait_ge(v_used, b * (tiles * TOPK) + (k * TOPK + NV))
                    dve.tensor_tensor(scaled, g.psum2(1), g.rows[:, 0 if t < NX else 1, 2], ALU.mult).then_inc(summed, 1)
                    dve.wait_ge(summed, b * tiles + (k + 1))
                    link(dve.tensor_tensor(g.x[:, t], g.x[:, t], scaled, ALU.add))

                link(dve.memset(g.psum2(1), 0.0))
                link.reset()
                each_head(dve, body)
                update(PH - 1, tiles)
                link.reset()

            @block.tensor
            def _(pe):
                pe.sem_inc(v_used, NV)
                every = (tiles - 2) * TOPK // (2 * KD)

                def scores(b, k):
                    if not exists(b, k):
                        return
                    head, t = b + k // tiles, k % tiles
                    if k == tiles:
                        pe.wait_ge(q_copied, b * 2 + 4)
                    if not (isinstance(b, int) and b * tiles + k < 2):
                        pe.wait_ge(ranked, b * (2 * tiles) + 2 * (k - 1))
                    for p in range(2):
                        last = pe.matmul(g.ps[:, k % 2, p * P:(p + 1) * P], q_t[:, p, t * P:(t + 1) * P],
                                         keys_t[:, bass.ds(head * 2 + p, 1)].rearrange("p c n -> p (c n)"),
                                         start=True, stop=True)
                    last.then_inc(scored, 1)

                def project(b, n):
                    c, k = divmod(n, KD)
                    if k == 0:
                        pe.wait_ge(slab_loaded[c], b * 16 + 16)
                        pe.wait_ge(q_copied, b * 2 + 2)
                    contract(c, k, 0)

                def contract(c, k, start):
                    bounds = sorted({start, 512, tiles * P})
                    for lo, hi in zip(bounds, bounds[1:]):
                        last = pe.matmul(g.psum2(2 + c)[:, lo:hi], slab[:, c, k], ht[:, k, lo:hi],
                                         start=(k == 0), stop=(k == KD - 1))
                    if k == KD - 1:
                        last.then_inc(q_done, 1)

                scores(0, 0)
                scores(0, 1)
                for c in range(2):
                    for k in range(KD):
                        contract(c, k, rest)
                pe.wait_ge(q_copied, 2)

                def body(b):
                    for k in range(tiles):
                        scores(b, k + 2)
                        pe.wait_ge(summed, b * tiles + (k + 1))
                        for j in range(TOPK):
                            f = k * TOPK + j
                            pe.wait_ge(v_loaded[j % NV], b * (16 * tiles * TOPK // NV) + 16 * (f // NV + 1))
                            pe.wait_ge(diag_ready, b * (tiles * TOPK) + (f + 1))
                            for c in range(2):
                                last = pe.matmul(g.psum2(1)[:, c * 512:(c + 1) * 512], diag[:, j % NDIAG],
                                                 v_at[j % NV][:, c * 512:(c + 1) * 512], start=(j == 0),
                                                 stop=(j == TOPK - 1))
                            last.then_inc(v_used, 1)
                            if exists(b, tiles) and f % every == every - 1 and f // every < 2 * KD:
                                project(b, f // every)

                each_head(pe, body)


@phase
def final_norm(g):
    nc, a = g.nc, g.a
    row_loaded, squared, mean_ready, rstd_ready, tile_ready, stored = g.sems(
        "f", "row_loaded", "squared", "mean_ready", "rstd_ready", "tile_ready", "stored")
    with ExitStack() as s:
        sb = lambda n, shape: s.enter_context(nc.sbuf_tensor(n, shape, F32))
        grow, y, stat = sb("final_row", [P, D]), sb("final", [P, NX, D]), sb("final_stat", [P, 3, NX])
        with nc.Block() as block:
            @block.sync
            def _(sp):
                sp.dma_start(grow[:], a["final_norm_g"].partition_broadcast(P)).then_inc(row_loaded, 16)
                for t in range(NX):
                    sp.wait_ge(tile_ready, t + 1)
                    sp.dma_start(a["out"][0, t * P:(t + 1) * P, :], y[:, t]).then_inc(stored, 16)
                sp.wait_ge(stored, 16 * NX)

            @block.scalar
            def _(act):
                for t in range(NX):
                    act.activation(y[:, t], g.x[:, t], ACT.Square, accum_out=stat[:, 0, t:t + 1]).then_inc(squared, 1)

            @block.gpsimd
            def _(pool):
                pool.wait_ge(mean_ready, 1)
                pool.tensor_tensor(stat[:, 2], stat[:, 1], g.half[:, 0:NX], ALU.pow).then_inc(rstd_ready, 1)

            @block.vector
            def _(dve):
                dve.wait_ge(squared, NX)
                dve.tensor_scalar(stat[:, 1], stat[:, 0], 1.0 / D, EPS, ALU.mult, ALU.add).then_inc(mean_ready, 1)
                dve.wait_ge(rstd_ready, 1)
                dve.wait_ge(row_loaded, 16)
                for t in range(NX):
                    dve.scalar_tensor_tensor(y[:, t], g.x[:, t], stat[:, 2, t:t + 1], grow[:], ALU.mult, ALU.mult
                                             ).then_inc(tile_ready, 1)


def trunk(nc, a):
    with ExitStack() as stack:
        g = Program(nc, stack, a)
        modulation(g)
        for l in range(DEPTH):
            last_layer = l == DEPTH - 1
            with ExitStack() as s:
                sb = lambda n, shape: s.enter_context(nc.sbuf_tensor(f"{n}_{l}", shape, F32))
                k_t = sb("k_t", [P, 2, TOK])
                cat = sb("cat", [P, KD, NX * P if last_layer else TOK])
                with ExitStack() as s2:
                    proj = s2.enter_context(nc.sbuf_tensor(f"proj_{l}", [P, NPROJ, TOK], F32))
                    with (nc.sbuf_tensor(f"h1_{l}", [P, NT, D], F32) as h,
                          nc.sbuf_tensor(f"h1_t_{l}", [P, KD, TOK], F32) as ht,
                          nc.sbuf_tensor(f"in_slab_{l}", [P, 2, KD, P], F32) as slab):
                        norm_and_project(g, l, 0, NT, h, {"h_t": ht, "slab": slab, "proj": proj, "k_t": k_t})
                    mix(g, l, proj, k_t, cat)
            tiles = NX if last_layer else NT
            with ExitStack() as s:
                sb = lambda n, shape: s.enter_context(nc.sbuf_tensor(f"{n}_{l}", shape, F32))
                h = sb("h2", [P, tiles, D])
                ht = sb("h_t", [P, KD, tiles * P])
                q_t = sb("peer_q_t", [P, 2, tiles * P])
                keys_t = sb("keys_t", [P, 2 * PH, P])
                slab = sb("q_slab", [P, 2, KD, P])
                norm_and_project(g, l, 1, tiles, h, {"h_t": ht, "slab": slab, "proj": q_t, "keys_t": keys_t})
                peer(g, l, tiles, h, ht, slab, q_t, keys_t)
        final_norm(g)


_INS = ["x", "c", "ctx", "c_ctx", "w_mod", "b_mod", "norm1_g", "norm2_g", "w_in", "w_out", "conv_a_w", "conv_b_w",
        "conv_b_bias", "conv_b_ln_g", "conv_b_ln_b", "mla_q_norm_g", "w_uq", "mla_kv_norm_g", "w_ukv", "peer_w_q",
        "peer_sub_keys", "peer_u", "peer_v", "final_norm_g"]


def shape_constants():
    axis = ROPE // 2
    inv = (ROPE_BASE ** (-np.arange(0, axis, 2, dtype=np.float32) / axis)).astype(np.float32)
    n = np.arange(SEQ)
    ar = (n // GRID_W).astype(np.float32)[:, None] * inv
    ac = (n % GRID_W).astype(np.float32)[:, None] * inv
    ang = np.concatenate([ar, ar, ac, ac], axis=-1).T
    sign = np.tile(np.repeat([-1.0, 1.0], ROPE // 4), 2)[:, None]
    tables = np.concatenate([np.cos(ang), sign * np.sin(ang)]).astype(np.float32)
    return {"identity": np.eye(P, dtype=np.float32), "rope_tables": np.ascontiguousarray(tables)}


def kernel(**inputs):
    import concourse.bacc as _bacc
    from concourse.bass_utils import run_bass_kernel_spmd as _run

    nc = _bacc.Bacc("TRN2", target_bir_lowering=False, num_devices=1)
    arrays, args = {}, {}
    host = {n: np.ascontiguousarray(inputs[n]) for n in _INS}
    host["peer_w_q"] = np.ascontiguousarray(
        host["peer_w_q"].reshape(DEPTH, KD, P, 2 * PH, P).transpose(0, 3, 2, 1, 4))
    host["peer_sub_keys"] = np.ascontiguousarray(
        host["peer_sub_keys"].reshape(DEPTH, 2 * PH, NKEY, P).transpose(0, 3, 1, 2))
    turned = np.arange(ROPE).reshape(2, 2, ROPE // 4)[:, ::-1].reshape(-1)
    uq = host["w_uq"].reshape(DEPTH, -1, HEADS, QK)
    host["w_uq"] = np.ascontiguousarray(np.concatenate([uq, uq[..., NOPE + turned]], -1).reshape(DEPTH, -1, HEADS * P))
    host["w_in"] = np.ascontiguousarray(np.concatenate([host["w_in"], host["w_in"][..., KRCHUNK * P + turned]], -1))
    host.update(shape_constants())
    for name, v in host.items():
        arrays[f"in_{name}"] = v
        args[name] = nc.dram_tensor(f"in_{name}", v.shape, mybir.dt.from_np(v.dtype), kind="ExternalInput").ap()
    args["out"] = nc.dram_tensor("out_0", (1, SEQ, D), F32, kind="ExternalOutput").ap()
    trunk(nc, args)
    r = _run(nc, [arrays], core_ids=[0])
    return r.results[0]["out_0"]
```
